# Optimizing a Trainium2 kernel written in Bass

```python
import jax, jax.numpy as jnp
from jax import lax
import numpy as np

D_MODEL = 1024
BATCH = 1
SEQ = 2048
DEPTH = 1
DEC_BATCH = 1
DEC_SEQ = 64
PAST_LEN = 512

CHUNK = 64
N_HEADS = 8
HEAD_DIM = 64
ATTN_DIM = N_HEADS * HEAD_DIM
CONV_DIM = D_MODEL - ATTN_DIM
CONV_GROUPS = 8
CONV_W = 3
D_FF = 4 * D_MODEL
Q_BLOCK = 128
EPS = 1e-6
NEG_INF = -1e30
PROJ_DIM = 3 * ATTN_DIM + N_HEADS + 3 * CONV_DIM

kernel_name = "hymba_fox_shortconv_streaming_step"

def rms_norm(x, g):
    xf = x.astype(jnp.float32)
    y = xf * lax.rsqrt(jnp.mean(xf * xf, axis=-1, keepdims=True) + EPS)
    return (y * g.astype(jnp.float32)).astype(x.dtype)

def project(h, w_in, b_f):
    b, t = h.shape[0], h.shape[1]
    z = h @ w_in
    cuts = [ATTN_DIM, 2 * ATTN_DIM, 3 * ATTN_DIM, 3 * ATTN_DIM + N_HEADS,
            3 * ATTN_DIM + N_HEADS + CONV_DIM, 3 * ATTN_DIM + N_HEADS + 2 * CONV_DIM]
    q, k, v, f, gate_b, gate_c, u = jnp.split(z, cuts, axis=-1)
    q = q.reshape(b, t, N_HEADS, HEAD_DIM)
    k = k.reshape(b, t, N_HEADS, HEAD_DIM)
    v = v.reshape(b, t, N_HEADS, HEAD_DIM)
    logf = jax.nn.log_sigmoid((f + b_f).astype(jnp.float32))
    return q, k, v, logf, gate_b, gate_c * u

def fox_attend(q, k, v, cq, ck, pos_q, pos_k):
    scale = HEAD_DIM ** -0.5
    s = jnp.einsum('bqhd,bkhd->bhqk', q, k).astype(jnp.float32) * scale
    decay = jnp.transpose(cq, (0, 2, 1))[:, :, :, None] - jnp.transpose(ck, (0, 2, 1))[:, :, None, :]
    mask = pos_k[None, :] <= pos_q[:, None]
    s = jnp.where(mask[None, None], s + decay, NEG_INF)
    p = jax.nn.softmax(s, axis=-1)
    return jnp.einsum('bhqk,bkhd->bqhd', p.astype(v.dtype), v)

def fox_prompt(q, k, v, logf):
    b, t = q.shape[0], q.shape[1]
    c = jnp.cumsum(logf.astype(jnp.float32), axis=1)
    nb = t // Q_BLOCK
    qb = q.reshape(b, nb, Q_BLOCK, N_HEADS, HEAD_DIM).transpose(1, 0, 2, 3, 4)
    cb = c.reshape(b, nb, Q_BLOCK, N_HEADS).transpose(1, 0, 2, 3)
    pb = jnp.arange(t, dtype=jnp.int32).reshape(nb, Q_BLOCK)
    pos_k = jnp.arange(t, dtype=jnp.int32)
    out = lax.map(lambda a: fox_attend(a[0], k, v, a[1], c, a[2], pos_k), (qb, cb, pb))
    return out.transpose(1, 0, 2, 3, 4).reshape(b, t, N_HEADS, HEAD_DIM)

def fox_sample(q, k, v, logf, past_k, past_v, past_logf):
    p_len, t = past_k.shape[1], q.shape[1]
    k_all = jnp.concatenate([past_k, k], axis=1)
    v_all = jnp.concatenate([past_v, v], axis=1)
    logf_all = jnp.concatenate([past_logf.astype(jnp.float32), logf.astype(jnp.float32)], axis=1)
    c = jnp.cumsum(logf_all, axis=1)
    pos_k = jnp.arange(p_len + t, dtype=jnp.int32)
    pos_q = p_len + jnp.arange(t, dtype=jnp.int32)
    return fox_attend(q, k_all, v_all, c[:, p_len:], c, pos_q, pos_k)

def short_conv(cu, prev, w):
    t = cu.shape[1]
    up = jnp.concatenate([prev.astype(cu.dtype), cu], axis=1)
    y = w[0] * up[:, 0:t]
    for j in range(1, CONV_W):
        y = y + w[j] * up[:, j:j + t]
    return y, up[:, up.shape[1] - (CONV_W - 1):]

def trunk_layer(x, conv_prev, attn_fn, g_pre_mix, w_in, b_f, conv_w, g_attn_out, g_conv_out,
                w_o, g_post_mix, g_pre_mlp, w_up, w_down, g_post_mlp):
    b, t = x.shape[0], x.shape[1]
    h = rms_norm(x, g_pre_mix)
    q, k, v, logf, gate_b, cu = project(h, w_in, b_f)
    o_attn = attn_fn(q, k, v, logf).reshape(b, t, ATTN_DIM)
    yc, conv_state = short_conv(cu, conv_prev, conv_w)
    o_conv = gate_b * yc
    merged = jnp.concatenate([rms_norm(o_attn, g_attn_out), rms_norm(o_conv, g_conv_out)], axis=-1)
    x = x + rms_norm(merged @ w_o, g_post_mix)
    h2 = rms_norm(x, g_pre_mlp)
    m = jnp.square(jax.nn.relu(h2 @ w_up)) @ w_down
    x = x + rms_norm(m, g_post_mlp)
    return x, k, v, logf, conv_state

def setup_inputs(seed: int = 0) -> dict:
    key = jax.random.key(seed)
    ks = jax.random.split(key, 24)
    f32 = jnp.float32
    nrm = lambda k, s, sc: jax.random.normal(k, s, f32) * sc
    gain = lambda k, s: 1.0 + 0.05 * jax.random.normal(k, s, f32)
    return {
        "x_prompt": nrm(ks[0], (BATCH, SEQ, D_MODEL), 1.0),
        "x_sample": nrm(ks[1], (DEC_BATCH, DEC_SEQ, D_MODEL), 1.0),
        "cache_k": nrm(ks[2], (DEPTH, DEC_BATCH, PAST_LEN, N_HEADS, HEAD_DIM), 1.0),
        "cache_v": nrm(ks[3], (DEPTH, DEC_BATCH, PAST_LEN, N_HEADS, HEAD_DIM), 1.0),
        "cache_logf": jax.nn.log_sigmoid(jax.random.uniform(ks[4], (DEPTH, DEC_BATCH, PAST_LEN, N_HEADS), f32, 1.0, 5.0)
                                          + jax.random.normal(ks[5], (DEPTH, DEC_BATCH, PAST_LEN, N_HEADS), f32)),
        "state_conv": nrm(ks[6], (DEPTH, DEC_BATCH, CONV_W - 1, CONV_DIM), 1.0),
        "g_pre_mix": gain(ks[7], (DEPTH, D_MODEL)),
        "w_in": nrm(ks[8], (DEPTH, D_MODEL, PROJ_DIM), D_MODEL ** -0.5),
        "b_f": jax.random.uniform(ks[9], (DEPTH, N_HEADS), f32, 1.0, 5.0),
        "conv_w": nrm(ks[10], (DEPTH, CONV_W, CONV_DIM), CONV_W ** -0.5),
        "g_attn_out": gain(ks[11], (DEPTH, ATTN_DIM)),
        "g_conv_out": gain(ks[12], (DEPTH, CONV_DIM)),
        "w_o": nrm(ks[13], (DEPTH, D_MODEL, D_MODEL), D_MODEL ** -0.5),
        "g_post_mix": gain(ks[14], (DEPTH, D_MODEL)),
        "g_pre_mlp": gain(ks[15], (DEPTH, D_MODEL)),
        "w_up": nrm(ks[16], (DEPTH, D_MODEL, D_FF), D_MODEL ** -0.5),
        "w_down": nrm(ks[17], (DEPTH, D_FF, D_MODEL), D_FF ** -0.5),
        "g_post_mlp": gain(ks[18], (DEPTH, D_MODEL)),
    }

def reference(x_prompt, x_sample, cache_k, cache_v, cache_logf, state_conv,
              g_pre_mix, w_in, b_f, conv_w, g_attn_out, g_conv_out, w_o,
              g_post_mix, g_pre_mlp, w_up, w_down, g_post_mlp):
    xp, xs = x_prompt, x_sample
    zero_conv = jnp.zeros((x_prompt.shape[0], CONV_W - 1, CONV_DIM), x_prompt.dtype)
    kp, vp, fp, cp = [], [], [], []
    ksl, vsl, fsl, csl = [], [], [], []
    for l in range(DEPTH):
        params = (g_pre_mix[l], w_in[l], b_f[l], conv_w[l], g_attn_out[l], g_conv_out[l],
                  w_o[l], g_post_mix[l], g_pre_mlp[l], w_up[l], w_down[l], g_post_mlp[l])
        xp, k1, v1, f1, c1 = trunk_layer(xp, zero_conv, fox_prompt, *params)
        pk, pv, pf = cache_k[l], cache_v[l], cache_logf[l]
        samp_fn = lambda q, k, v, lf, pk=pk, pv=pv, pf=pf: fox_sample(q, k, v, lf, pk, pv, pf)
        xs, k2, v2, f2, c2 = trunk_layer(xs, state_conv[l], samp_fn, *params)
        kp.append(k1); vp.append(v1); fp.append(f1); cp.append(c1)
        ksl.append(k2); vsl.append(v2); fsl.append(f2); csl.append(c2)
    return (xp, xs,
            jnp.stack(kp), jnp.stack(vp), jnp.stack(fp), jnp.stack(cp),
            jnp.stack(ksl), jnp.stack(vsl), jnp.stack(fsl), jnp.stack(csl))


_drawn_inputs = setup_inputs


def setup_inputs(seed=0):
    import zlib

    import numpy as np

    out = dict(_drawn_inputs(seed))
    spreads = {}
    factors = {}
    for name, (base, spread) in spreads.items():
        noise = np.random.default_rng([zlib.crc32(name.encode()), seed]).standard_normal(out[name].shape)
        drawn = base * np.exp(spread * noise) if base else spread * noise
        out[name] = __import__('jax').numpy.asarray(drawn.astype(out[name].dtype))
    for name, factor in factors.items():
        out[name] = (out[name] * factor).astype(out[name].dtype)
    return out
```

```python
import concourse.bass as bass
from concourse import mybir
from contextlib import ExitStack

F32 = mybir.dt.float32
F32R = mybir.dt.float32r
ALU = mybir.AluOpType
ACT = mybir.ActivationFunctionType
AX = mybir.AxisListType

P = 128
D = 1024
SEQ = 2048
DEC = 64
PAST = 512
ROWS = SEQ + DEC
HEADS = 8
HD = 64
AD = HEADS * HD
CD = D - AD
CONV_W = 3
FF = 4 * D
PROJ = 3 * AD + HEADS + 3 * CD
EPS = 1e-6
NEG = -1e30

KB = D // P
QT = SEQ // P
RT = QT + 1
MT = 6
MN = ROWS // MT
CJ = CD // P
CB = PAST // P
LB = QT + CB + 1
LKEYS = QT * P + PAST + DEC



def rows_of(tile):
    return P if tile < QT else DEC


def project_inputs(nc, io, dr, sem, ident):
    ctx = ExitStack()
    with ctx:
        def sb(name, shape, dt=F32):
            return ctx.enter_context(nc.sbuf_tensor(name, shape, dt))

        h_hi = sb("h_hi", [P, KB, ROWS], F32R)
        h_lo = sb("h_lo", [P, KB, ROWS], F32R)
        w_raw = sb("w_raw", [P, KB, P])
        w_hi = sb("w_hi", [P, 3, KB, P], F32R)
        w_lo = sb("w_lo", [P, 3, KB, P], F32R)
        zw = ROWS + 2 * 2
        z = sb("z", [P, 3, zw])
        nat = sb("nat", [P, 2, 4, P])
        g_mix = sb("g_mix", [P, D])
        x_extra = sb("x_extra", [P, D])
        par_rows = sb("par_rows", [24, P])
        par = sb("par", [P, 6, CJ])
        cwj = sb("cwj", [P, 6])
        tails = sb("tails", [P, 4, CJ])
        tail_rows = sb("tail_rows", [4 * CJ, P])
        b_f = sb("b_f", [HEADS, 1])
        ssq = sb("ssq", [P, RT])
        std = sb("std", [P, RT])
        rstd = sb("rstd", [P, RT])
        lf = sb("lf", [P, LB, HEADS])
        fz = sb("fz", [P, RT * HEADS])
        f_e = sb("f_e", [P, RT * HEADS])
        f_w = sb("f_w", [P, RT * HEADS])
        f_ln = sb("f_ln", [P, RT * HEADS])
        f_m = sb("f_m", [P, RT * HEADS])
        before = sb("before", [P, LB, HEADS])
        ncum = sb("ncum", [P, LB * HEADS])
        ncum_t = sb("ncum_t", [P, 2, P])
        upper = sb("upper", [P, P])
        ones = sb("ones", [P, P])
        x_in = [z[:, 1, 0:D], z[:, 1, D:2 * D], x_extra[:, :]]
        h_rows = [z[:, 2, 0:D], z[:, 2, D:2 * D]]
        junk = [z[:, 0, 0:D], z[:, 0, D:2 * D]]
        bank = [ctx.enter_context(nc.psum_tensor(f"proj{i}", [P, 512], F32)) for i in range(8)]
        h_bank = [bank[6], bank[7]]

        x_ready = [sem(f"x_ready{i}") for i in range(3)]
        par_ready = sem("par_ready")
        par_rows_t = sem("par_rows_t")
        par_done = sem("par_done")
        consts = sem("proj_consts")
        ssq_done = sem("ssq_done")
        var_done = sem("var_done")
        std_done = sem("std_done")
        rstd_done = sem("rstd_done")
        h_done = sem("h_done")
        h_turned = sem("h_turned")
        h_hi_done = sem("h_hi_done")
        h_lo_done = sem("h_lo_done")
        w_loaded = sem("w_loaded")
        w_split = sem("w_split")
        w_hi_done = sem("w_hi_done")
        mm_done = sem("mm_done")
        bank_free = sem("bank_free")
        nat_turned = sem("nat_turned")
        nat_free = sem("nat_free")
        nat_stored = [sem(f"nat_stored{i}") for i in range(2)]
        qk_stored = [sem(f"qk_stored{i}") for i in range(2)]
        f_turned = sem("f_turned")
        f_chain = sem("f_chain")
        f_act = sem("f_act")
        lf_done = sem("lf_done")
        lf_cached = sem("lf_cached")
        lf_stored = sem("lf_stored")
        cum_done = sem("cum_done")
        ncum_done = sem("ncum_done")
        ncum_turned = sem("ncum_turned")
        ncum_out = sem("ncum_out")
        ncum_stored = sem("ncum_stored")
        conv_chain = sem("conv_chain")
        conv_stored = sem("conv_stored")
        tail_turned = sem("tail_turned")
        tail_done = sem("tail_done")
        tail_stored = sem("tail_stored")

        w_view = io["w_in"].rearrange("o (k p) c -> (o p) k c", p=P)
        F_COL = 3 * AD
        B_COL = F_COL + HEADS
        C_COL = B_COL + CD
        U_COL = C_COL + CD
        QKV_BLOCK, CONV_BLOCK = 1, 1 + 3 * CJ
        TURNS = [range(0, 4), range(4, 8), range(8, 12), range(12, 15), range(15, RT)]
        block = ctx.enter_context(nc.Block())

        @block.sync
        def _(sp):
            def load_x(t):
                if t >= 3:
                    sp.wait_ge(h_done, t - 2)
                src = io["x_prompt"][0, t * P:(t + 1) * P, :] if t < QT else io["x_sample"][0]
                sp.dma_start(x_in[t % 3][0:rows_of(t), :], src).then_inc(x_ready[t % 3], 16)

            def load_w(m, col):
                if not isinstance(m, int) or m > 0:
                    sp.wait_ge(w_split, m)
                sp.dma_start(w_raw[:, :, :], w_view[:, :, bass.ds(col, P)]).then_inc(w_loaded, 16)

            sp.dma_start(g_mix[:, :], io["g_pre_mix"].to_broadcast([P, D])).then_inc(par_ready, 16)
            load_x(0)
            load_x(1)
            load_w(0, F_COL)
            sp.dma_start(par_rows[0:12, :], io["conv_w"].rearrange("o w (j p) -> (o w j) p", p=P)).then_inc(par_ready, 16)
            sp.dma_start(par_rows[12:16, :], io["g_conv_out"].rearrange("o (j p) -> (o j) p", p=P)).then_inc(par_ready, 16)
            sp.dma_start(par_rows[16:24, :], io["state_conv"].rearrange("o b w (j p) -> (o b w j) p", p=P)).then_inc(par_ready, 16)
            sp.dma_start(b_f[:, :], io["b_f"].rearrange("o h -> h o")).then_inc(par_ready, 16)
            for t in range(2, RT):
                load_x(t)
            sp.wait_ge(consts, 1)
            sp.dma_start(lf[:, QT:QT + CB, :], io["cache_logf"][0, 0].rearrange("(a p) h -> p a h", p=P)).then_inc(lf_cached, 16)
            with sp.Fori(0, CJ) as j:
                for i in range(3):
                    load_w(QKV_BLOCK + 3 * j + i, i * AD + j * P)
            with sp.Fori(0, CJ) as j:
                for i, col in enumerate((C_COL, U_COL, B_COL)):
                    load_w(CONV_BLOCK + 3 * j + i, col + j * P)

        @block.gpsimd
        def _(pool):
            pool.memset(lf[:, :, :], 0.0).then_inc(consts, 1)
            pool.memset(ones[:, :], 1.0).then_inc(consts, 1)
            pool.memset(ident[:, :], 0.0).then_inc(consts, 1)
            pool.wait_ge(consts, 3)
            pool.affine_select(out=ident[:, :], in_=ident[:, :], compare_op=ALU.not_equal, fill=1.0, base=0,
                               pattern=[[-1, P]], channel_multiplier=1).then_inc(consts, 1)
            pool.affine_select(out=upper[:, :], in_=ones[:, :], compare_op=ALU.is_ge, fill=0.0, base=0,
                               pattern=[[1, P]], channel_multiplier=-1).then_inc(consts, 1)

            def split_rest(m, slot):
                pool.wait_ge(w_hi_done, m + 1)
                pool.tensor_tensor(w_lo[:, slot], w_raw[:, :, :], w_hi[:, slot].bitcast(F32), ALU.subtract).then_inc(w_split, 1)

            split_rest(0, 0)
            with pool.Fori(0, 2 * CJ) as j:
                for i in range(3):
                    split_rest(QKV_BLOCK + 3 * j + i, (1 + i) % 3)

        @block.scalar
        def _(act):
            def square(t):
                act.wait_ge(x_ready[t % 3], 16 * (t // 3 + 1))
                n = rows_of(t)
                act.activation(junk[t % 2][0:n, :], x_in[t % 3][0:n, :], ACT.Square, accum_out=ssq[0:n, t:t + 1]).then_inc(ssq_done, 1)

            def h_part(t):
                n = rows_of(t)
                for b in range(2):
                    act.wait_ge(h_turned, 2 * t + b + 1)
                    act.activation(h_hi[:, 4 * b:4 * b + 4, t * P:t * P + n],
                                   h_bank[b][:, :].rearrange("p (k n) -> p k n", k=4)[:, :, 0:n],
                                   ACT.Copy).then_inc(h_hi_done, 1)

            square(0)
            act.wait_ge(par_rows_t, 1)
            act.activation(par[:, :, :].rearrange("p a j -> p (a j)"), bank[5][:, 0:24], ACT.Copy).then_inc(par_done, 1)
            for t in range(RT):
                if t + 1 < RT:
                    square(t + 1)
                act.wait_ge(var_done, t + 1)
                n = rows_of(t)
                act.activation(std[0:n, t:t + 1], std[0:n, t:t + 1], ACT.Sqrt).then_inc(std_done, 1)
                if t >= 1:
                    h_part(t - 1)
            h_part(RT - 1)
            act.wait_ge(f_chain, 3)
            act.activation(f_e[:, :], f_m[:, :], ACT.Exp, scale=-1.0).then_inc(f_act, 1)
            act.wait_ge(f_chain, 4)
            act.activation(f_ln[:, :], f_w[:, :], ACT.Ln).then_inc(f_act, 1)
            act.wait_ge(lf_done, 1)
            act.dma_start(io["logf_prompt"][0, 0].rearrange("(a p) h -> p a h", p=P), lf[:, 0:QT, :]).then_inc(lf_stored, 16)
            act.dma_start(io["logf_sample"][0, 0], lf[0:DEC, LB - 1, :]).then_inc(lf_stored, 16)

            def take_rows(j, i):
                prompt, sample = (io["k_prompt"], io["k_sample"]) if i == 1 else (io["v_prompt"], io["v_sample"])
                for g in range(5):
                    s = ((i - 1) * 5 + g) % 2
                    seen = (i - 1) * 5 + g
                    act.wait_ge(nat_turned, 10 * j + seen + 1)
                    if not isinstance(j, int) or seen >= 2:
                        split_before = 1 if seen > (4, 9)[s] else 0
                        act.wait_ge(nat_stored[s], 16 * (6 * j + seen // 2 + split_before))
                    src = bank[6 + s][:, :].rearrange("p (a f) -> p a f", a=4)
                    tiles = [t for t in TURNS[g] if t < QT]
                    n = len(tiles)
                    copy = act.activation(nat[:, s, 0:n], src[:, 0:n], ACT.Copy)
                    if g == 4:
                        copy = act.activation(nat[0:DEC, s, n], src[0:DEC, n], ACT.Copy)
                    copy.then_inc(nat_free, 1)
                    act.wait_ge(nat_free, 2 + 10 * j + seen + 1)
                    act.dma_start(prompt[0, 0].rearrange("(a p) h d -> p a (h d)", p=P)[:, tiles[0]:tiles[0] + n, bass.ds(j * P, P)],
                                  nat[:, s, 0:n]).then_inc(nat_stored[s], 16)
                    if g == 4:
                        act.dma_start(sample[0, 0].rearrange("t h d -> t (h d)")[:, bass.ds(j * P, P)],
                                      nat[0:DEC, s, n]).then_inc(nat_stored[s], 16)

            def qkv_out(j):
                m = QKV_BLOCK + 3 * j
                act.wait_ge(bank_free, MT + MT * (m + 1))
                act.dma_start(dr["q_t"][bass.ds(j * P, P), :], z[:, 0, 0:ROWS]).then_inc(qk_stored[0], 16)
                act.wait_ge(bank_free, MT + MT * (m + 2))
                act.dma_start(dr["k_t"][bass.ds(j * P, P), :], z[:, 1, 0:ROWS]).then_inc(qk_stored[1], 16)
                take_rows(j, 1)

            qkv_out(0)
            with act.Fori(1, CJ) as j:
                take_rows(j - 1, 2)
                qkv_out(j)
            take_rows(CJ - 1, 2)
            act.wait_ge(ncum_turned, 1)
            act.activation(ncum_t[:, 0], bank[6][:, 0:P], ACT.Copy).then_inc(ncum_out, 1)
            act.activation(ncum_t[0:(CB + 1) * HEADS, 1], bank[7][0:(CB + 1) * HEADS, 0:P], ACT.Copy).then_inc(ncum_out, 1)
            act.wait_ge(ncum_out, 2)
            for b in range(QT):
                act.dma_start(dr["ncum"][:, b * P:(b + 1) * P], ncum_t[b * HEADS:(b + 1) * HEADS, 0]).then_inc(ncum_stored, 16)
            for b in range(CB):
                act.dma_start(dr["ncum"][:, SEQ + b * P:SEQ + (b + 1) * P], ncum_t[b * HEADS:(b + 1) * HEADS, 1]).then_inc(ncum_stored, 16)
            act.dma_start(dr["ncum"][:, SEQ + PAST:LKEYS], ncum_t[CB * HEADS:(CB + 1) * HEADS, 1, 0:DEC]).then_inc(ncum_stored, 16)
            with act.Fori(0, CJ) as j:
                act.wait_ge(bank_free, MT + MT * (CONV_BLOCK + 3 * j + 3))
                act.dma_start(dr["conv_t"][bass.ds(j * P, P), 0:SEQ], z[:, 2, 2:2 + SEQ]).then_inc(conv_stored, 16)
                act.dma_start(dr["conv_t"][bass.ds(j * P, P), SEQ:ROWS], z[:, 2, 4 + SEQ:4 + ROWS]).then_inc(conv_stored, 16)
            act.wait_ge(tail_turned, 1)
            act.activation(tail_rows[:, :], bank[6][0:4 * CJ, 0:P], ACT.Copy).then_inc(tail_done, 1)
            act.wait_ge(tail_done, 1)
            act.dma_start(io["conv_prompt"].rearrange("o b w (j p) -> (o b w j) p", p=P), tail_rows[0:2 * CJ, :]).then_inc(tail_stored, 16)
            act.dma_start(io["conv_sample"].rearrange("o b w (j p) -> (o b w j) p", p=P), tail_rows[2 * CJ:4 * CJ, :]).then_inc(tail_stored, 16)
            act.wait_ge(tail_stored, 32)
            act.wait_ge(conv_stored, 32 * CJ)
            act.wait_ge(ncum_stored, 16 * LB)
            act.wait_ge(lf_stored, 32)
            for s in range(2):
                act.wait_ge(qk_stored[s], 16 * CJ)
                act.wait_ge(nat_stored[s], 16 * 6 * CJ)

        @block.vector
        def _(dve):
            dve.sem_inc(bank_free, MT)
            dve.sem_inc(nat_free, 2)

            def variance(t):
                dve.wait_ge(ssq_done, t + 1)
                n = rows_of(t)
                dve.tensor_scalar(std[0:n, t:t + 1], ssq[0:n, t:t + 1], 1.0 / D, EPS, ALU.mult, ALU.add).then_inc(var_done, 1)

            def normalise(t):
                n = rows_of(t)
                dve.wait_ge(std_done, t + 1)
                dve.reciprocal(rstd[0:n, t:t + 1], std[0:n, t:t + 1]).then_inc(rstd_done, 1)
                dve.wait_ge(rstd_done, t + 1)
                if t >= 2:
                    dve.wait_ge(h_turned, 2 * (t - 1))
                dve.scalar_tensor_tensor(h_rows[t % 2][0:n, :], x_in[t % 3][0:n, :], rstd[0:n, t:t + 1], g_mix[0:n, :],
                                         ALU.mult, ALU.mult).then_inc(h_done, 1)

            def h_rest(t):
                n = rows_of(t)
                for b in range(2):
                    dve.wait_ge(h_hi_done, 2 * t + b + 1)
                    part = (slice(None), slice(4 * b, 4 * b + 4), slice(t * P, t * P + n))
                    dve.tensor_tensor(h_lo[part], h_bank[b][:, :].rearrange("p (k n) -> p k n", k=4)[:, :, 0:n],
                                      h_hi[part].bitcast(F32), ALU.subtract).then_inc(h_lo_done, 1)

            def take(m, i, put, ahead=True):
                if ahead:
                    dve.wait_ge(w_loaded, 16 * (m + 2))
                    dve.tensor_copy(w_hi[:, (i + 1) % 3], w_raw[:, :, :]).then_inc(w_hi_done, 1)
                for n in range(MT):
                    dve.wait_ge(mm_done, MT * m + n + 1)
                    put(n)[-1].then_inc(bank_free, 1)

            dve.wait_ge(w_loaded, 16)
            dve.tensor_copy(w_hi[:, 0], w_raw[:, :, :]).then_inc(w_hi_done, 1)
            dve.wait_ge(par_ready, 16 * 5)
            variance(0)
            for t in range(RT):
                if t + 1 < RT:
                    variance(t + 1)
                normalise(t)
                if t >= 1:
                    h_rest(t - 1)
            h_rest(RT - 1)
            take(0, 0, lambda n: [dve.tensor_scalar(z[0:HEADS, 0, n * MN:(n + 1) * MN], bank[n][0:HEADS, 0:MN], b_f[:, :], None, ALU.add)])
            n_f = RT * HEADS
            full = QT * HEADS
            dve.wait_ge(f_turned, 1)
            dve.memset(fz[DEC:P, full:n_f], 0.0)
            dve.tensor_copy(fz[:, 0:full], bank[6][:, 0:full])
            dve.tensor_copy(fz[0:DEC, full:n_f], bank[6][0:DEC, full:n_f]).then_inc(f_chain, 1)
            dve.wait_ge(f_chain, 1)
            dve.tensor_scalar(f_m[:, :], fz[:, :], -1.0, None, ALU.mult).then_inc(f_chain, 1)
            dve.wait_ge(f_chain, 2)
            dve.tensor_tensor(f_m[:, :], f_m[:, :], fz[:, :], ALU.max).then_inc(f_chain, 1)
            dve.wait_ge(f_act, 1)
            dve.tensor_scalar(f_w[:, :], f_e[:, :], 1.0, None, ALU.add).then_inc(f_chain, 1)
            dve.wait_ge(f_chain, 4)
            dve.scalar_tensor_tensor(f_e[:, :], f_w[:, :], -1.0, f_e[:, :], ALU.add, ALU.subtract).then_inc(f_chain, 1)
            dve.wait_ge(f_act, 2)
            dve.reciprocal(f_m[:, :], f_w[:, :]).then_inc(f_chain, 1)
            dve.wait_ge(f_chain, 6)
            dve.tensor_tensor(f_e[:, :], f_e[:, :], f_m[:, :], ALU.mult).then_inc(f_chain, 1)
            dve.wait_ge(f_chain, 7)
            dve.tensor_tensor(f_e[:, :], f_e[:, :], f_ln[:, :], ALU.subtract).then_inc(f_chain, 1)
            dve.wait_ge(f_chain, 8)
            dve.wait_ge(lf_cached, 16)
            lf_new = lf[:, 0:QT, :].rearrange("p a h -> p (a h)")
            dve.scalar_tensor_tensor(lf_new, fz[:, 0:full], 0.0, f_e[:, 0:full], ALU.min, ALU.add)
            dve.scalar_tensor_tensor(lf[0:DEC, LB - 1, :], fz[0:DEC, full:n_f], 0.0, f_e[0:DEC, full:n_f], ALU.min, ALU.add).then_inc(lf_done, 1)

            def qkv(j, first):
                m = QKV_BLOCK + 3 * j
                if not first:
                    dve.wait_ge(qk_stored[0], 16 * j)
                take(m, 1, lambda n: [dve.tensor_scalar(z[:, 0, n * MN:(n + 1) * MN], bank[n][:, 0:MN], HD ** -0.5, None, ALU.mult)])
                if not first:
                    dve.wait_ge(qk_stored[1], 16 * j)
                    dve.wait_ge(nat_turned, 10 * j - 5)
                take(m + 1, 2, lambda n: [dve.tensor_copy(z[:, 1, n * MN:(n + 1) * MN], bank[n][:, 0:MN])])
                if not first:
                    dve.wait_ge(nat_turned, 10 * j)
                take(m + 2, 0, lambda n: [dve.tensor_copy(z[:, 2, n * MN:(n + 1) * MN], bank[n][:, 0:MN])])

            dve.wait_ge(f_turned, 1)
            qkv(0, True)
            with dve.Fori(1, CJ) as j:
                qkv(j, False)

            def cumulate():
                dve.wait_ge(cum_done, 1)
                total = bank[7][:, 0:LB * HEADS].rearrange("p (a h) -> p a h", h=HEADS)
                dve.memset(before[:, 0, :], 0.0)
                dve.memset(before[:, QT, :], 0.0).then_inc(ncum_done, 1)
                done = 1
                for b in range(1, LB):
                    if b != QT:
                        dve.wait_ge(ncum_done, done)
                        dve.tensor_tensor(before[:, b, :], before[:, b - 1, :], total[:, b - 1, :], ALU.add).then_inc(ncum_done, 1)
                        done += 1
                dve.wait_ge(ncum_done, done)
                dve.scalar_tensor_tensor(ncum[:, :], bank[6][:, 0:LB * HEADS], -1.0, before[:, :, :].rearrange("p a h -> p (a h)"),
                                         ALU.mult, ALU.subtract).then_inc(ncum_done, 1)

            def conv(j, first, j_last=False):
                m = CONV_BLOCK + 3 * j
                dve.wait_ge(par_done, 1)
                dve.tensor_copy(cwj[:, :], par[:, :, bass.ds(j, 1)].rearrange("p a j -> p (a j)")).then_inc(conv_chain, 1)
                if first:
                    dve.wait_ge(qk_stored[0], 16 * CJ)
                take(m, 1, lambda n: [dve.tensor_copy(z[:, 0, n * MN:(n + 1) * MN], bank[n][:, 0:MN])])
                if first:
                    cumulate()
                    dve.wait_ge(qk_stored[1], 16 * CJ)
                    dve.wait_ge(nat_turned, 10 * CJ)
                last = SEQ - (MT - 1) * MN

                def gate(n):
                    if n < MT - 1:
                        return [dve.tensor_tensor(z[:, 1, 2 + n * MN:2 + (n + 1) * MN], bank[n][:, 0:MN], z[:, 0, n * MN:(n + 1) * MN], ALU.mult)]
                    return [dve.tensor_tensor(z[:, 1, 2 + n * MN:2 + SEQ], bank[n][:, 0:last], z[:, 0, n * MN:SEQ], ALU.mult),
                            dve.tensor_tensor(z[:, 1, 4 + SEQ:4 + ROWS], bank[n][:, last:MN], z[:, 0, SEQ:ROWS], ALU.mult)]

                dve.wait_ge(bank_free, MT + MT * (m + 1))
                dve.wait_ge(conv_chain, 4 * j + 1)
                dve.memset(z[:, 1, 0:2], 0.0)
                dve.tensor_copy(z[:, 1, 2 + SEQ:4 + SEQ], cwj[:, 4:6])
                take(m + 1, 2, gate)
                dve.wait_ge(bank_free, MT + MT * (m + 2))
                dve.tensor_copy(tails[:, 0:2, bass.ds(j, 1)].rearrange("p a j -> p (a j)"), z[:, 1, SEQ:SEQ + 2])
                dve.tensor_copy(tails[:, 2:4, bass.ds(j, 1)].rearrange("p a j -> p (a j)"), z[:, 1, 2 + ROWS:4 + ROWS])
                if not first:
                    dve.wait_ge(conv_stored, 32 * j)
                y = z[:, 2, 2:zw]
                dve.tensor_scalar(y, z[:, 1, 0:zw - 2], cwj[:, 0:1], None, ALU.mult).then_inc(conv_chain, 1)
                dve.wait_ge(conv_chain, 4 * j + 2)
                dve.scalar_tensor_tensor(y, z[:, 1, 1:zw - 1], cwj[:, 1:2], y, ALU.mult, ALU.add).then_inc(conv_chain, 1)
                dve.wait_ge(conv_chain, 4 * j + 3)
                dve.scalar_tensor_tensor(y, z[:, 1, 2:zw], cwj[:, 2:3], y, ALU.mult, ALU.add).then_inc(conv_chain, 1)
                dve.wait_ge(conv_chain, 4 * j + 4)

                def gate_out(n):
                    if n < MT - 1:
                        at = z[:, 2, 2 + n * MN:2 + (n + 1) * MN]
                        return [dve.tensor_tensor(at, bank[n][:, 0:MN], at, ALU.mult)]
                    prompt, sample = z[:, 2, 2 + n * MN:2 + SEQ], z[:, 2, 4 + SEQ:4 + ROWS]
                    return [dve.tensor_tensor(prompt, bank[n][:, 0:last], prompt, ALU.mult),
                            dve.tensor_tensor(sample, bank[n][:, last:MN], sample, ALU.mult)]

                take(m + 2, 0, gate_out, ahead=not j_last)

            conv(0, True)
            with dve.Fori(1, CJ - 1) as j:
                conv(j, False)
            conv(CJ - 1, False, True)

        @block.tensor
        def _(pe):
            def multiply(m, slot, n):
                pe.wait_ge(bank_free, MT * m + n + 1)
                if n == 0:
                    pe.wait_ge(w_split, m + 1)
                rows = slice(n * MN, (n + 1) * MN)
                for k in range(KB):
                    for i, (w, h) in enumerate(((w_hi, h_hi), (w_hi, h_lo), (w_lo, h_hi))):
                        mm = pe.matmul(bank[n][:, 0:MN], w[:, slot, k], h[:, k, rows], start=(k == 0 and i == 0), stop=(k == KB - 1 and i == 2))
                mm.then_inc(mm_done, 1)

            def turn(j, i, g):
                m = QKV_BLOCK + 3 * j + i
                seen = (i - 1) * len(TURNS) + g
                pe.wait_ge(nat_free, 10 * j + seen + 1)
                tiles = TURNS[g]
                pe.wait_ge(bank_free, MT + MT * m + min(MT, (tiles[-1] * P + P - 1) // MN + 1))
                for t in tiles:
                    n = rows_of(t)
                    tr = pe.transpose(bank[6 + seen % 2][0:n, (t - tiles[0]) * P:(t - tiles[0] + 1) * P], z[:, i, t * P:t * P + n], ident[:, :])
                tr.then_inc(nat_turned, 1)

            def block_of(m, slot, between=None):
                for n in range(MT):
                    multiply(m, slot, n)
                    if between and n < len(TURNS):
                        turn(*between, n)

            pe.wait_ge(par_ready, 16 * 5)
            pe.wait_ge(consts, 5)
            pe.transpose(bank[5][:, 0:24], par_rows[:, :], ident[0:24, 0:24]).then_inc(par_rows_t, 1)
            pe.wait_ge(par_done, 1)

            done = 0
            for t in range(RT):
                n = rows_of(t)
                pe.wait_ge(h_done, t + 1)
                for b in range(2):
                    if t >= 1:
                        pe.wait_ge(h_lo_done, 2 * t - 1 + b)
                    for k in range(4):
                        tr = pe.transpose(h_bank[b][:, k * P:k * P + n], h_rows[t % 2][0:n, (4 * b + k) * P:(4 * b + k + 1) * P], ident[0:n, 0:n])
                    tr.then_inc(h_turned, 1)
                ready = t * P if t < RT - 1 else 0
                while done < MT - 1 and (done + 1) * MN <= ready:
                    pe.wait_ge(h_lo_done, 2 * t)
                    multiply(0, 0, done)
                    done += 1
            pe.wait_ge(h_lo_done, 2 * RT)
            while done < MT:
                multiply(0, 0, done)
                done += 1
            pe.wait_ge(bank_free, 2 * MT)
            for t in range(RT):
                n = rows_of(t)
                tr = pe.transpose(bank[6][0:n, t * HEADS:(t + 1) * HEADS], z[0:HEADS, 0, t * P:t * P + n], ident[0:HEADS, 0:HEADS])
            tr.then_inc(f_turned, 1)
            block_of(QKV_BLOCK, 1)
            pe.wait_ge(lf_done, 1)
            block_of(QKV_BLOCK + 1, 2)
            block_of(QKV_BLOCK + 2, 0, (0, 1))
            with pe.Fori(1, CJ) as j:
                m = QKV_BLOCK + 3 * j
                block_of(m, 1, (j - 1, 2))
                block_of(m + 1, 2)
                block_of(m + 2, 0, (j, 1))
            block_of(CONV_BLOCK, 1, (CJ - 1, 2))
            pe.wait_ge(nat_free, 2 + 10 * CJ)
            lf_all = lf[:, :, :].rearrange("p a h -> p (a h)")
            pe.matmul(bank[6][:, 0:LB * HEADS], upper[:, :], lf_all, start=True, stop=True)
            pe.matmul(bank[7][:, 0:LB * HEADS], ones[:, :], lf_all, start=True, stop=True).then_inc(cum_done, 1)
            block_of(CONV_BLOCK + 1, 2)
            pe.wait_ge(ncum_done, LB)
            pe.transpose(bank[6][:, 0:P], ncum[:, 0:P], ident[:, :])
            pe.transpose(bank[7][0:(CB + 1) * HEADS, 0:P], ncum[:, P:LB * HEADS], ident[:, :]).then_inc(ncum_turned, 1)
            block_of(CONV_BLOCK + 2, 0)
            with pe.Fori(1, CJ) as j:
                m = CONV_BLOCK + 3 * j
                block_of(m, 1)
                block_of(m + 1, 2)
                block_of(m + 2, 0)
            pe.wait_ge(ncum_out, 2)
            pe.wait_ge(bank_free, MT + MT * (CONV_BLOCK + 3 * CJ))
            pe.transpose(bank[6][0:4 * CJ, 0:P], tails[:, :, :].rearrange("p a j -> p (a j)"), ident[:, :]).then_inc(tail_turned, 1)


S_BANKS, T_BANKS, O_BANKS = 3, 3, 1
PREPARE_IN = 2
V_BEHIND = 2
B_AHEAD, B_SLOWER = 3, 0.9
DELAY = {"act": {"M": 6, "T": 1, "C": 1, "O": 2}, "dve": {"M": 1, "T": 2, "C": 2}}


def queue_of(steps, engine):
    delay = DELAY.get(engine, {})
    places = sorted(range(len(steps)), key=lambda n: (n + delay.get(steps[n].kind, 0), n))
    return [steps[n] for n in places]


class Step:

    def __init__(self, kind, par, off, tile=None, n=None, col=None, width=None, g=None, blocks=None, cols=None,
                 t=None, first=False, last=False, v=None, o=None):
        self.kind, self.par, self.off = kind, par, off
        self.tile, self.n, self.col, self.width = tile, n, col, width
        self.g, self.blocks, self.cols = g, blocks, cols
        self.t, self.first, self.last = t, first, last
        self.v, self.o = v, o
        self.at, self.free, self.exps, self.last_piece, self.c_before = None, None, None, None, None


def attention_order():
    extra = QT // 4

    def scores(par, off, g):
        steps = [Step("C", par, off)] if g == 0 else []
        for tile in [*range(4 * g, 4 * g + 4)] + ([QT] if g == 0 else []):
            if tile < QT:
                pieces = [(c, min(512, (tile + 1) * P - c)) for c in range(0, (tile + 1) * P, 512)]
            else:
                pieces = [(0, PAST), (PAST, DEC)]
            for n, (col, width) in enumerate(pieces):
                steps.append(Step("S", par, off, tile=tile, n=n, col=col, width=width))
            steps.append(Step("M", par, off, tile=tile, n=len(pieces)))
        return steps

    def products(par, off, g):
        steps, behind = [], []
        if g == extra:
            units = [(tuple(range(CB)), 0), ((CB,), 0)]
        else:
            units = [((j,), max(0, j - 4 * g) * P) for j in range(4 * g + 4)]
        for n, (blocks, col) in enumerate(units):
            cols = slice(col, 512) if g < extra else slice(0, len(blocks) * P)
            t = Step("T", par, off, g=g, blocks=blocks, cols=cols)
            steps.append(t)
            behind.append(Step("V", par, off, g=g, t=t, first=n == 0, last=n == len(units) - 1))
            if len(behind) > V_BEHIND:
                steps.append(behind.pop(0))
        return steps + behind + [Step("O", par, off, g=g, v=behind[-1])]

    def mix(a, b):
        out, i, j = [], 0, 0
        while i < len(a) or j < len(b):
            if j >= len(b) or (i < len(a) and (i + B_AHEAD) * len(b) <= j * len(a) * B_SLOWER):
                out.append(a[i])
                i += 1
            else:
                out.append(b[j])
                j += 1
        return out

    def prepare(par, off):
        return [Step("H", par, off, n=n) for n in range(3)]

    before = [Step("L", 0, 0)] + prepare(0, 0) + scores(0, 0, 0)
    body, late = [], None
    for par in range(2):
        for g in range(extra):
            parts = []
            for q in [g, extra] if g == 0 else [g]:
                steps = products(par, par, q)
                if late:
                    steps.insert(4, late)
                parts += steps
                late = Step("N", par, par, g=q, o=steps[-1])
            if g == 0:
                body.append(Step("L", 1 - par, par + 1))
            if g == PREPARE_IN:
                parts[2:2] = [Step("H", 1 - par, par + 1, n=0)]
                parts[8:8] = [Step("H", 1 - par, par + 1, n=1)]
                parts[14:14] = [Step("H", 1 - par, par + 1, n=2)]
            body += mix(parts, scores(par, par, g + 1) if g + 1 < extra else scores(1 - par, par + 1, 0))
    body.append(late)

    def group_of(tile):
        return extra if tile == QT else tile // 4

    count = dict.fromkeys("LHCSMTVON", 0)
    turned_by = {}
    exps_by = {}
    for x in before + body:
        kind = x.kind
        if x is body[0]:
            start = dict(count)
            turned_by[1] = count["T"]
        x.at = count[kind]
        count[kind] += 1
        if x.kind == "M":
            x.last_piece = count["S"] - 1
            exps_by[x.off, group_of(x.tile)] = count["M"]
        if x.kind == "S" and x.n == 0 and x.tile % 4 == 0 and x.tile < QT:
            x.free = turned_by.get((x.tile // 4) % 2)
        if x.kind == "T":
            x.exps = exps_by[x.off, x.g]
            turned_by[0 if x.g == extra else x.g % 2] = count["T"]
    per = {k: count[k] - start[k] for k in count}
    return before, body, start, per


def attend(nc, io, dr, sem, ident):
    ctx = ExitStack()
    with ctx:
        def sb(name, shape, dt=F32):
            return ctx.enter_context(nc.sbuf_tensor(name, shape, dt))

        QW = RT * P
        KW = ROWS + PAST
        NV = QT + 1 + CB
        k_raw = sb("k_raw", [P, ROWS])
        q_raw = sb("q_raw", [P, ROWS])
        v_raw = sb("v_raw", [P, NV, HD])
        c_raw = sb("c_raw", [P, CB, 2, HD])
        k_hl = [sb(f"k_hl{i}", [P, KW], F32R) for i in range(2)]
        q_hi = [sb(f"q_hi{i}", [P, QW], F32R) for i in range(2)]
        q_lo = [sb(f"q_lo{i}", [P, QW], F32R) for i in range(2)]
        v_hl = [sb(f"v_hl{i}", [P, NV, 2 * HD], F32R) for i in range(2)]
        nck = [sb(f"nck{i}", [P, LKEYS]) for i in range(2)]
        sets = [sb("scores_a", [P, 4 * 1536]), sb("scores_b", [P, 4 * 2048])]
        p_hi = sb("p_hi", [P, T_BANKS, 512], F32R)
        p_lo = sb("p_lo", [P, T_BANKS, 512], F32R)
        o_t = sb("o_t", [P, 2, 512])
        att = sb("att", [P, 2, 4, HD])
        fold = sb("fold", [P, HD])
        ident_r = sb("ident_r", [P, P], F32R)
        mask = sb("mask", [P, P])
        mask_r = sb("mask_r", [P, P], F32R)
        maxes = sb("maxes", [P, 34, 4])
        nmax = sb("nmax", [P, 34])
        total = sb("total", [P, 34])
        rtotal = sb("rtotal", [P, 34])
        s_bank = [ctx.enter_context(nc.psum_tensor(f"s_bank{i}", [P, 512], F32)) for i in range(S_BANKS)]
        t_bank = [ctx.enter_context(nc.psum_tensor(f"t_bank{i}", [P, 512], F32)) for i in range(T_BANKS)]
        o_bank = [ctx.enter_context(nc.psum_tensor(f"o_bank{i}", [P, 512], F32)) for i in range(O_BANKS)]
        n_bank = ctx.enter_context(nc.psum_tensor("n_bank", [P, 512], F32))

        consts = sem("att_consts")
        rounded = sem("att_rounded")
        q_loaded, k_loaded, c_loaded = sem("q_loaded"), sem("k_loaded"), sem("c_raw_loaded")
        v_loaded = sem("v_loaded")
        nck_loaded = [sem(f"nck_loaded{i}") for i in range(2)]
        head_hi = sem("head_hi")
        head_lo = sem("head_lo")
        scored = sem("scored")
        taken = sem("taken")
        max_done = sem("max_done")
        nmax_done = sem("nmax_done")
        exp_done = sem("exp_done")
        turned = sem("turned")
        c_turned = sem("c_turned")
        c_hi_done = sem("c_hi_done")
        c_lo_done = sem("c_lo_done")
        hi_done = sem("hi_done")
        lo_done = sem("lo_done")
        used = sem("used")
        o_taken = sem("o_taken")
        in_rows = sem("in_rows")
        recip_done = sem("recip_done")
        att_done = sem("att_done")
        att_stored = [sem(f"att_stored{i}") for i in range(2)]

        before, body, start, per = attention_order()
        QM = per["M"]
        EXTRA = QT // 4

        def tile_at(tile):
            if tile == QT:
                return sets[0][:, 2048:2048 + PAST + P]
            g, i = tile // 4, tile % 4
            pitch = 512 * (g + 1)
            return sets[g % 2][:, i * pitch:i * pitch + (tile + 1) * P]

        def upto(kind, it, n):
            return per[kind] * it + n

        def loop(eng, name, step):
            for x in queue_of(before, name):
                step(0, x)
            with eng.Fori(0, HEADS // 2) as it:
                for x in queue_of(body, name):
                    step(it, x)

        m_of = {}
        for x in before + body:
            if x.kind == "M":
                m_of[x.off, x.tile] = x.at % QM
        o_of = {(x.off, x.g): x.at for x in body if x.kind == "O"}
        n_before, c_last = {}, None
        n_count = 0
        for x in before + body:
            if x.kind == "C":
                n_before[x.off], c_last = n_count, x.off
            if x.kind == "N":
                x.c_before, n_count = c_last, n_count + 1
        s_last = {x.off: x.at for x in before + body if x.kind == "S"}
        block = ctx.enter_context(nc.Block())

        @block.sync
        def _(sp):
            s_read = {0: 0, 1: start["S"], 2: s_last[0] + 1}

            def step(it, x):
                if x.kind == "N":
                    rows = slice(0, P) if x.g < EXTRA else slice(0, DEC)
                    n = 4 if x.g < EXTRA else 1
                    sp.wait_ge(att_done, 1 + upto("N", it, x.at) + 1)
                    dst = dr["attn"][x.g * 4 * P:(x.g * 4 + n) * P, :] if n == 4 else dr["attn"][SEQ:ROWS, :]
                    sp.dma_start(dst.rearrange("(a p) c -> p a c", a=n)[:, :, bass.ds((2 * it + x.off) * HD, HD)],
                                 att[rows, x.at % 2, 0:n, :]).then_inc(att_stored[x.at % 2], 16)
                if x.kind != "L":
                    return
                n = 2 * it + x.off
                h = n if isinstance(n, int) else sp.snap(n % HEADS)
                sp.wait_ge(head_lo, 3 * n)
                lines = bass.ds(h * HD, HD)
                for half in range(2):
                    sp.dma_start(q_raw[half * HD:half * HD + HD, :], dr["q_t"][lines, :]).then_inc(q_loaded, 16)
                for half in range(2):
                    sp.dma_start(k_raw[half * HD:half * HD + HD, :], dr["k_t"][lines, :]).then_inc(k_loaded, 16)
                def load_v():
                    sp.dma_start(v_raw[:, 0:QT, :], io["v_prompt"][0, 0].rearrange("(a p) h d -> p a (h d)", p=P)[:, :, lines]).then_inc(v_loaded, 16)
                    sp.dma_start(v_raw[0:DEC, QT, :], io["v_sample"][0, 0].rearrange("t h d -> t (h d)")[:, lines]).then_inc(v_loaded, 16)
                    sp.dma_start(v_raw[:, QT + 1:NV, :], io["cache_v"][0, 0].rearrange("(a p) h d -> p a (h d)", p=P)[:, :, lines]).then_inc(v_loaded, 16)

                if not isinstance(n, int):
                    load_v()
                sp.wait_ge(c_turned, n)
                for half in range(2):
                    sp.dma_start(c_raw[:, :, half, :], io["cache_k"][0, 0].rearrange("(a p) h d -> p a (h d)", p=P)[:, :, lines]).then_inc(c_loaded, 16)
                sp.wait_ge(taken, S_BANKS + upto("S", it, s_read[x.off]))
                sp.dma_start(nck[x.par][:, :], dr["ncum"][bass.ds(h, 1), :].to_broadcast([P, LKEYS])).then_inc(nck_loaded[x.par], 16)
                if isinstance(n, int):
                    sp.wait_ge(consts, 10)
                    load_v()

            for i in range(2):
                sp.sem_inc(att_stored[i], 16)
            loop(sp, "sync", step)
            for i in range(2):
                sp.wait_ge(att_stored[i], 16 * (1 + per["N"] // 2 * (HEADS // 2)))
            sp.wait_ge(nck_loaded[0], 16 * (HEADS // 2 + 1))
            for loaded in (q_loaded, k_loaded, c_loaded):
                sp.wait_ge(loaded, 32 * (HEADS + 1))
            sp.wait_ge(v_loaded, 16 * 3 * (HEADS + 1))

        def rest_of_head(eng, par, which):
            if which == 0:
                return eng.tensor_tensor(q_lo[par][:, 0:ROWS], q_raw[:, :], q_hi[par][:, 0:ROWS].bitcast(F32), ALU.subtract)
            if which == 1:
                low = slice(HD, P)
                return eng.tensor_tensor(k_hl[par][low, 0:ROWS], k_raw[low, :], k_hl[par][low, 0:ROWS].bitcast(F32), ALU.subtract)
            return eng.tensor_tensor(v_hl[par][:, :, HD:], v_raw[:, :, :], v_hl[par][:, :, 0:HD].bitcast(F32), ALU.subtract)

        @block.gpsimd
        def _(pool):
            pool.memset(v_raw[:, QT, :], 0.0).then_inc(consts, 1)
            for i in range(2):
                pool.memset(q_hi[i][:, ROWS:].bitcast(F32), 0.0).then_inc(consts, 1)
                pool.memset(q_lo[i][:, ROWS:].bitcast(F32), 0.0).then_inc(consts, 1)
            pool.memset(mask[:, :], 0.0).then_inc(consts, 1)
            pool.memset(fold[:, :], 0.0).then_inc(consts, 1)
            pool.wait_ge(consts, 7)
            pool.affine_select(out=mask[:, :], in_=mask[:, :], compare_op=ALU.is_ge, fill=NEG, base=0,
                               pattern=[[-1, P]], channel_multiplier=1).then_inc(consts, 1)
            pool.affine_select(out=fold[:, :], in_=fold[:, :], compare_op=ALU.not_equal, fill=1.0, base=0,
                               pattern=[[-1, HD]], channel_multiplier=1).then_inc(consts, 1)
            pool.wait_ge(consts, 9)
            pool.affine_select(out=fold[:, :], in_=fold[:, :], compare_op=ALU.not_equal, fill=1.0, base=-HD,
                               pattern=[[-1, HD]], channel_multiplier=1).then_inc(consts, 1)

            def step(it, x):
                if x.kind != "H" or isinstance(it, int):
                    return
                par, n = x.par, 2 * it + x.off
                pool.wait_ge(head_hi, 3 * n + x.n + 1)
                pool.wait_ge(head_lo, 3 * n + x.n)
                rest_of_head(pool, par, x.n).then_inc(head_lo, 1)

            loop(pool, "pool", step)

        @block.scalar
        def _(act):
            act.sem_inc(o_taken, O_BANKS)
            act.wait_ge(consts, 10)
            act.activation(ident_r[:, :], ident[:, :], ACT.Copy)
            act.activation(mask_r[:, :], mask[:, :], ACT.Copy).then_inc(rounded, 1)
            v_read = {0: 0, 1: 0, 2: per["V"] // 2}

            def step(it, x):
                par = x.par
                if x.kind == "H":
                    n = 2 * it + x.off
                    if x.n == 0:
                        act.wait_ge(used, T_BANKS + upto("V", it, v_read[x.off]))
                        act.wait_ge(q_loaded, 32 * (n + 1))
                        act.activation(q_hi[par][:, 0:ROWS], q_raw[:, :], ACT.Copy).then_inc(head_hi, 1)
                    elif x.n == 1:
                        act.wait_ge(k_loaded, 32 * (n + 1))
                        act.activation(k_hl[par][:, 0:ROWS], k_raw[:, :], ACT.Copy).then_inc(head_hi, 1)
                    else:
                        act.wait_ge(v_loaded, 16 * 3 * (n + 1))
                        act.activation(v_hl[par][:, :, 0:HD], v_raw[:, :, :], ACT.Copy).then_inc(head_hi, 1)
                elif x.kind == "C":
                    act.wait_ge(c_turned, 2 * it + x.off + 1)
                    act.activation(k_hl[par][:, ROWS:KW], n_bank[:, :], ACT.Copy).then_inc(c_hi_done, 1)
                elif x.kind == "M":
                    m = x.at % QM
                    at = tile_at(x.tile) if x.tile < QT else tile_at(QT)[:, 0:PAST + DEC]
                    act.wait_ge(nmax_done, upto("M", it, x.at) + 1)
                    act.activation(at, at, ACT.Exp, bias=nmax[:, m:m + 1], accum_out=total[:, m:m + 1]).then_inc(exp_done, 1)
                elif x.kind == "T":
                    act.wait_ge(turned, 1 + upto("T", it, x.at) + 1)
                    act.wait_ge(used, upto("V", it, x.at) + 1)
                    act.activation(p_hi[:, x.at % T_BANKS, x.cols], t_bank[x.at % T_BANKS][:, x.cols], ACT.Copy).then_inc(hi_done, 1)
                elif x.kind == "O":
                    width = P if x.g == EXTRA else 512
                    act.wait_ge(used, T_BANKS + upto("V", it, x.v.at) + 1)
                    act.wait_ge(in_rows, upto("O", it, x.at) + 1)
                    act.activation(o_t[:, x.at % 2, 0:width], o_bank[x.at % O_BANKS][:, 0:width], ACT.Copy).then_inc(o_taken, 1)

            loop(act, "act", step)

        @block.vector
        def _(dve):
            dve.sem_inc(taken, S_BANKS)
            dve.sem_inc(lo_done, T_BANKS)
            dve.sem_inc(att_done, 1)
            pieces = dve.alloc_register("pieces")
            dve.reg_mov(pieces, 1)

            def step(it, x):
                par = x.par
                if x.kind == "H" and isinstance(it, int):
                    dve.wait_ge(head_hi, x.n + 1)
                    rest_of_head(dve, par, x.n).then_inc(head_lo, 1)
                elif x.kind == "C":
                    low = slice(HD, P)
                    dve.wait_ge(c_hi_done, 2 * it + x.off + 1)
                    dve.tensor_tensor(k_hl[par][low, ROWS:KW], n_bank[low, :], k_hl[par][low, ROWS:KW].bitcast(F32),
                                      ALU.subtract).then_inc(c_lo_done, 1)
                elif x.kind == "S":
                    m = m_of[x.off, x.tile]
                    if x.n == 0 and x.tile % 4 == 0 and x.tile < QT and x.free is not None:
                        dve.wait_ge(turned, 1 + upto("T", it, x.free))
                    if x.n == 0 and x.tile == 0:
                        dve.wait_ge(nck_loaded[par], 16 * (it + (2 if x.off == 2 else 1)))
                    if x.n == 1 and x.tile == QT:
                        dve.memset(tile_at(QT)[:, PAST + DEC:], 0.0)
                    key = x.col if x.tile < QT else SEQ + x.col
                    dve.wait_ge(scored, pieces)
                    dve.reg_add(pieces, pieces, 1)
                    dve.tensor_tensor_reduce(out=tile_at(x.tile)[:, x.col:x.col + x.width], in0=s_bank[x.at % S_BANKS][:, 0:x.width],
                                             in1=nck[par][:, key:key + x.width], scale=1.0, scalar=4 * NEG, op0=ALU.add, op1=ALU.max,
                                             accum_out=maxes[:, m, x.n:x.n + 1]).then_inc(taken, 1)
                elif x.kind == "M":
                    m = x.at % QM
                    dve.wait_ge(taken, S_BANKS + upto("S", it, x.last_piece) + 1)
                    dve.tensor_reduce(nmax[:, m:m + 1], maxes[:, m, 0:x.n], AX.X, ALU.max, negate=True).then_inc(nmax_done, 1)
                elif x.kind == "T":
                    dve.wait_ge(hi_done, upto("T", it, x.at) + 1)
                    dve.tensor_tensor(p_lo[:, x.at % T_BANKS, x.cols], t_bank[x.at % T_BANKS][:, x.cols], p_hi[:, x.at % T_BANKS, x.cols].bitcast(F32),
                                      ALU.subtract).then_inc(lo_done, 1)
                elif x.kind == "N":
                    n = 4 if x.g < EXTRA else 1
                    m = m_of[x.off, QT if n == 1 else 4 * x.g]
                    dve.reciprocal(rtotal[:, m:m + n], total[:, m:m + n]).then_inc(recip_done, 1)
                    dve.wait_ge(recip_done, upto("N", it, x.at) + 1)
                    dve.wait_ge(in_rows, 2 + upto("N", it, x.at) + 1)
                    dve.wait_ge(att_stored[x.at % 2], 16 * (per["N"] // 2 * it + x.at // 2 + 1))
                    dve.tensor_tensor(att[:, x.at % 2, 0:n, :], n_bank[:, 0:n * HD].rearrange("p (a d) -> p a d", d=HD),
                                      rtotal[:, m:m + n].rearrange("p (a o) -> p a o", o=1).to_broadcast([P, n, HD]), ALU.mult).then_inc(att_done, 1)

            loop(dve, "dve", step)

        @block.tensor
        def _(pe):
            pe.sem_inc(turned, 1)
            pe.sem_inc(used, T_BANKS)
            pe.sem_inc(in_rows, 2)
            pe.wait_ge(rounded, 1)

            def step(it, x):
                par, n_head = x.par, 2 * it + x.off
                if x.kind == "C":
                    pe.wait_ge(c_loaded, 32 * (n_head + 1))
                    if n_before[x.off]:
                        pe.wait_ge(att_done, 1 + upto("N", it, n_before[x.off]))
                    for a in range(CB):
                        tr = pe.transpose(n_bank[:, a * P:(a + 1) * P], c_raw[:, a].rearrange("p b d -> p (b d)"), ident[:, :])
                    tr.then_inc(c_turned, 1)
                elif x.kind == "S":
                    if x.n == 0 and x.tile == 0:
                        pe.wait_ge(head_lo, 3 * n_head + 2)
                    if x.n == 0 and x.tile == QT:
                        pe.wait_ge(c_lo_done, n_head + 1)
                    pe.wait_ge(taken, upto("S", it, x.at) + 1)
                    key = x.col if x.tile < QT else (ROWS if x.n == 0 else SEQ)
                    query = slice(x.tile * P, (x.tile + 1) * P)
                    out, keys = s_bank[x.at % S_BANKS][:, 0:x.width], k_hl[par][:, key:key + x.width]
                    diagonal = x.col + x.width == (x.tile + 1) * P if x.tile < QT else x.n == 1
                    pe.matmul(out, q_hi[par][:, query], keys, start=True, stop=False)
                    mm = pe.matmul(out, q_lo[par][:, query], keys, start=False, stop=not diagonal)
                    if diagonal:
                        w = min(x.width, P)
                        mm = pe.matmul(out[:, x.width - w:x.width], ident_r[:, :], mask_r[:, 0:w], start=False, stop=True)
                    mm.then_inc(scored, 1)
                elif x.kind == "T":
                    pe.wait_ge(exp_done, upto("M", it, x.exps))
                    pe.wait_ge(lo_done, upto("T", it, x.at) + 1)
                    bank = t_bank[x.at % T_BANKS]
                    if x.g < EXTRA:
                        j = x.blocks[0]
                        for i in range(x.cols.start // P, 4):
                            tr = pe.transpose(bank[:, i * P:(i + 1) * P], tile_at(4 * x.g + i)[:, j * P:(j + 1) * P], ident[:, :])
                    else:
                        for i, j in enumerate(x.blocks):
                            tr = pe.transpose(bank[:, i * P:(i + 1) * P], tile_at(QT)[:, j * P:(j + 1) * P], ident[:, :])
                    tr.then_inc(turned, 1)
                elif x.kind == "V":
                    t, o = x.t, o_of[x.off, x.g]
                    pe.wait_ge(lo_done, T_BANKS + upto("T", it, t.at) + 1)
                    if x.first:
                        pe.wait_ge(head_lo, 3 * n_head + 3)
                        pe.wait_ge(o_taken, upto("O", it, o) + 1)
                    for i, j in enumerate(t.blocks):
                        if x.g < EXTRA:
                            out, at, vb = o_bank[o % O_BANKS][:, t.cols], t.cols, j
                        else:
                            out, at, vb = o_bank[o % O_BANKS][:, 0:P], slice(i * P, (i + 1) * P), QT if j == CB else QT + 1 + j
                        pe.matmul(out, v_hl[par][:, vb, :], p_hi[:, t.at % T_BANKS, at], start=x.first and i == 0, stop=False)
                        mm = pe.matmul(out, v_hl[par][:, vb, :], p_lo[:, t.at % T_BANKS, at], start=False, stop=x.last and i == len(t.blocks) - 1)
                    mm.then_inc(used, 1)
                elif x.kind == "N":
                    pe.wait_ge(o_taken, O_BANKS + upto("N", it, x.at) + 1)
                    pe.wait_ge(att_done, upto("N", it, x.at) + 1)
                    if x.c_before is not None:
                        pe.wait_ge(c_lo_done, 2 * it + x.c_before + 1)
                    for i in range(4 if x.g < EXTRA else 1):
                        mm = pe.matmul(n_bank[:, i * HD:(i + 1) * HD], o_t[:, x.at % 2, i * P:(i + 1) * P], fold[:, :], start=True, stop=True)
                    mm.then_inc(in_rows, 1)

            loop(pe, "pe", step)


def mix_rows(nc, io, dr, sem, ident):
    ctx = ExitStack()
    with ctx:
        def sb(name, shape, dt=F32):
            return ctx.enter_context(nc.sbuf_tensor(name, shape, dt))

        w_hi = sb("wo_hi", [P, KB, D], F32R)
        w_lo = sb("wo_lo", [P, KB, D], F32R)
        w_raw = sb("wo_raw", [P, KB, D])
        g_attn = sb("g_attn", [P, AD])
        g_post = sb("g_post", [P, D])
        g_mlp = sb("g_mlp", [P, D])
        g_conv_rows = sb("g_conv_rows", [CJ, P])
        g_conv = sb("g_conv", [P, CJ])
        ones = sb("mix_ones", [P, 1])
        a_in = sb("a_in", [P, 2, AD])
        c_in = sb("c_in", [P, 2, CJ, P])
        x_in = sb("mx_in", [P, 2, D])
        ag = sb("ag", [P, AD])
        cg = sb("cg", [P, CJ, P])
        csq = sb("csq", [P, CJ, P])
        junk = sb("junk", [P, D])
        junk_a = sb("junk_a", [P, AD])
        a_hi = sb("a_hi", [P, 2, CJ, P], F32R)
        a_lo = sb("a_lo", [P, 2, CJ, P], F32R)
        c_hi = sb("c_hi", [P, 2, CJ, P], F32R)
        c_lo = sb("c_lo", [P, 2, CJ, P], F32R)
        part = sb("part", [P, D])
        mixed = sb("mixed", [P, D])
        scaled = sb("scaled", [P, D])
        x2 = sb("x2", [P, 2, D])
        h2 = sb("h2", [P, D])
        h2_hi = sb("h2_hi", [P, 2, KB, P], F32R)
        h2_lo = sb("h2_lo", [P, 2, KB, P], F32R)
        s_ac = sb("s_ac", [P, 2, 2])
        d_ac = sb("d_ac", [P, 2, 2])
        r_ac = sb("r_ac", [P, 2, 2])
        s_m, d_m, r_m = sb("s_m", [P, 1]), sb("d_m", [P, 1]), sb("r_m", [P, 1])
        s_2, d_2, r_2 = sb("s_2", [P, 1]), sb("d_2", [P, 1]), sb("r_2", [P, 1])
        a_bank = ctx.enter_context(nc.psum_tensor("a_bank", [P, D], F32))
        c_bank = ctx.enter_context(nc.psum_tensor("c_bank", [P, D], F32))
        t_bank = ctx.enter_context(nc.psum_tensor("at_bank", [P, 512], F32))
        q_bank = ctx.enter_context(nc.psum_tensor("q_bank", [P, 512], F32))
        h_bank = [ctx.enter_context(nc.psum_tensor(f"h_bank{i}", [P, 512], F32)) for i in range(2)]

        names = """w_hi_done w_lo_done g_loaded g_late_loaded g_rows_t g_conv_done ones_done
                   ag_done a_turned a_hi_done a_lo_done sq_a csq_done cg_done c_hi_done c_lo_done c_summed var_ac std_ac rstd_ac
                   a_mult c_mult part_done mixed_done sq_m var_m std_m rstd_m scaled_done x2_done sq_2 var_2 std_2 rstd_2
                   h2_done h2_turned h2_hi_done h2_lo_done""".split()
        S = {n: sem("mix_" + n) for n in names}
        a_loaded, c_loaded, x_loaded, x2_stored, h2_stored = ([sem(f"mix_{n}{i}") for i in range(2)]
                                                              for n in ("a_loaded", "c_loaded", "x_loaded", "x2_stored", "h2_stored"))
        w_loaded = [sem(f"mix_w_loaded{k}") for k in range(KB)]
        block = ctx.enter_context(nc.Block())
        w_view = io["w_o"].rearrange("o (k p) n -> (o p) k n", p=P)

        def at(t):
            return (t * P, rows_of(t)) if isinstance(t, int) else (t * P, P)

        def run(eng, step):
            for t in range(3):
                step(t, t % 2)
            with eng.Fori(0, 5) as i:
                step(2 * i + 3, 1)
                step(2 * i + 4, 0)
            for t in range(13, RT + 1):
                step(t, t % 2)

        def is_tile(t):
            return not isinstance(t, int) or 0 <= t < RT

        def half_of(t, s):
            return (t - s) * 8 + 16

        @block.sync
        def _(sp):
            def load_ac(t, s):
                row, n = at(t)
                if not isinstance(t, int) or t >= 2:
                    sp.wait_ge(S["ag_done"], t - 1)
                    sp.wait_ge(S["sq_a"], t - 1)
                    sp.wait_ge(S["cg_done"], t - 1)
                sp.dma_start(a_in[0:n, s, :], dr["attn"][bass.ds(row, n), :]).then_inc(a_loaded[s], 16)
                sp.dma_start(c_in[:, s, :, 0:n], dr["conv_t"].rearrange("(j p) r -> p j r", p=P)[:, :, bass.ds(row, n)]).then_inc(c_loaded[s], 16)

            def load_x(t, s):
                row, n = at(t)
                if not isinstance(t, int) or t >= 2:
                    sp.wait_ge(S["x2_done"], t - 1)
                src = io["x_sample"][0] if isinstance(t, int) and t == QT else io["x_prompt"][0, bass.ds(row, n), :]
                sp.dma_start(x_in[0:n, s, :], src).then_inc(x_loaded[s], 16)

            load_ac(0, 0)
            sp.dma_start(g_attn[:, :], io["g_attn_out"].to_broadcast([P, AD])).then_inc(S["g_loaded"], 16)
            sp.dma_start(g_conv_rows[:, :], io["g_conv_out"].rearrange("o (j p) -> (o j) p", p=P)).then_inc(S["g_loaded"], 16)
            for k in range(KB):
                sp.dma_start(w_raw[:, k, :], w_view[:, k, :]).then_inc(w_loaded[k], 16)
            load_ac(1, 1)
            sp.dma_start(g_post[:, :], io["g_post_mix"].to_broadcast([P, D])).then_inc(S["g_late_loaded"], 16)
            load_x(0, 0)
            sp.dma_start(g_mlp[:, :], io["g_pre_mlp"].to_broadcast([P, D])).then_inc(S["g_late_loaded"], 16)
            load_x(1, 1)

            def step(t, s):
                if is_tile(t + 2) and (not isinstance(t, int) or t + 2 < RT):
                    load_ac(t + 2, s)
                if not isinstance(t, int) or 1 <= t < RT - 1:
                    load_x(t + 1, 1 - s)

            run(sp, step)
            for s in range(2):
                n_tiles = (RT + 1 - s) // 2
                sp.wait_ge(x2_stored[s], 16 * n_tiles)
                sp.wait_ge(h2_stored[s], 32 * n_tiles)

        @block.gpsimd
        def _(pool):
            pool.memset(ones[:, :], 1.0).then_inc(S["ones_done"], 1)

            def front(t, s):
                pool.wait_ge(c_loaded[s], half_of(t, s))
                if not isinstance(t, int) or t >= 1:
                    pool.wait_ge(S["c_summed"], t)
                pool.tensor_tensor(csq[:, :, :], c_in[:, s], c_in[:, s], ALU.mult).then_inc(S["csq_done"], 1)
                pool.wait_ge(S["csq_done"], t + 1)
                if not isinstance(t, int) or t >= 1:
                    pool.wait_ge(S["c_lo_done"], t)
                pool.tensor_tensor(cg[:, :, :], c_in[:, s], g_conv[:, :].rearrange("p (j o) -> p j o", o=1).to_broadcast([P, CJ, P]),
                                   ALU.mult).then_inc(S["cg_done"], 1)
                pool.wait_ge(S["c_hi_done"], t + 1)
                pool.tensor_tensor(c_lo[:, s], cg[:, :, :], c_hi[:, s].bitcast(F32), ALU.subtract).then_inc(S["c_lo_done"], 1)

            pool.wait_ge(S["g_conv_done"], 1)
            front(0, 0)

            def step(t, s):
                if is_tile(t + 1):
                    front(t + 1, 1 - s)

            run(pool, step)

        @block.scalar
        def _(act):
            def w_first(k):
                act.wait_ge(w_loaded[k], 16)
                act.activation(w_hi[:, k, :], w_raw[:, k, :], ACT.Copy).then_inc(S["w_hi_done"], 1)

            def front_squares(t, s):
                act.wait_ge(a_loaded[s], half_of(t, s))
                if not isinstance(t, int) or t >= 2:
                    act.wait_ge(S["rstd_ac"], t - 1)
                act.activation(junk_a[:, :], a_in[:, s, :], ACT.Square, accum_out=s_ac[:, s, 0:1]).then_inc(S["sq_a"], 1)
                act.wait_ge(S["cg_done"], t + 1)
                if not isinstance(t, int) or t >= 2:
                    act.wait_ge(S["c_mult"], t - 1)
                act.activation(c_hi[:, s], cg[:, :, :], ACT.Copy).then_inc(S["c_hi_done"], 1)

            def front_turned(t, s):
                act.wait_ge(S["a_turned"], t + 1)
                if not isinstance(t, int) or t >= 2:
                    act.wait_ge(S["a_mult"], t - 1)
                act.activation(a_hi[:, s], t_bank[:, :].rearrange("p (j n) -> p j n", j=CJ), ACT.Copy).then_inc(S["a_hi_done"], 1)

            def front_root(t, s):
                act.wait_ge(S["var_ac"], t + 1)
                act.activation(d_ac[:, s, :], d_ac[:, s, :], ACT.Sqrt).then_inc(S["std_ac"], 1)

            def back_squares(t):
                act.wait_ge(S["mixed_done"], t + 1)
                act.activation(junk[:, :], mixed[:, :], ACT.Square, accum_out=s_m[:, :]).then_inc(S["sq_m"], 1)

            def back_root(t):
                act.wait_ge(S["var_m"], t + 1)
                act.activation(d_m[:, :], d_m[:, :], ACT.Sqrt).then_inc(S["std_m"], 1)

            def back_second(t, s):
                act.wait_ge(S["x2_done"], t + 1)
                act.activation(junk[:, :], x2[:, s, :], ACT.Square, accum_out=s_2[:, :]).then_inc(S["sq_2"], 1)
                row, n = at(t)
                act.dma_start(dr["x2"][bass.ds(row, n), :], x2[0:n, s, :]).then_inc(x2_stored[s], 16)
                act.wait_ge(S["var_2"], t + 1)
                act.activation(d_2[:, :], d_2[:, :], ACT.Sqrt).then_inc(S["std_2"], 1)

            def take_part(t, s):
                act.wait_ge(S["a_mult"], t + 1)
                act.wait_ge(S["rstd_ac"], t + 1)
                if not isinstance(t, int) or t >= 1:
                    act.wait_ge(S["mixed_done"], t)
                act.activation(part[:, :], a_bank[:, :], ACT.Copy, scale=r_ac[:, s, 0:1]).then_inc(S["part_done"], 1)

            def back_out(t, s):
                if not isinstance(t, int) or t >= 2:
                    act.wait_ge(h2_stored[s], 2 * (half_of(t, s) - 16))
                for b in range(2):
                    act.wait_ge(S["h2_turned"], 2 * t + b + 1)
                    act.activation(h2_hi[:, s, 4 * b:4 * b + 4], h_bank[b][:, :].rearrange("p (k n) -> p k n", k=4), ACT.Copy).then_inc(S["h2_hi_done"], 1)

            def store_h2(t, s):
                row, n = at(t)
                act.wait_ge(S["h2_lo_done"], 2 * t + 2)
                for part, name in ((h2_hi, "h2_hi"), (h2_lo, "h2_lo")):
                    act.dma_start(dr[name].rearrange("(k p) r -> p k r", p=P)[:, :, bass.ds(row, n)], part[:, s, :, 0:n].bitcast(F32)).then_inc(h2_stored[s], 16)

            act.wait_ge(S["g_rows_t"], 1)
            act.activation(g_conv[:, :], q_bank[:, 64:64 + CJ], ACT.Copy).then_inc(S["g_conv_done"], 1)
            w_first(0)
            front_squares(0, 0)
            w_first(1)
            front_turned(0, 0)
            front_root(0, 0)
            for k in range(2, KB):
                w_first(k)

            def step(t, s):
                last, nxt = not isinstance(t, int) or t >= 1, is_tile(t + 1)
                if nxt:
                    front_squares(t + 1, 1 - s)
                if last:
                    back_squares(t - 1)
                    back_root(t - 1)
                if nxt:
                    front_turned(t + 1, 1 - s)
                    front_root(t + 1, 1 - s)
                if last:
                    back_second(t - 1, 1 - s)
                if is_tile(t):
                    take_part(t, s)
                if not isinstance(t, int) or t >= 2:
                    store_h2(t - 2, s)
                if last:
                    back_out(t - 1, 1 - s)

            run(act, step)
            store_h2(RT - 1, (RT - 1) % 2)

        @block.vector
        def _(dve):
            def scale_rows(t, s):
                dve.wait_ge(a_loaded[s], half_of(t, s))
                if not isinstance(t, int) or t >= 1:
                    dve.wait_ge(S["a_turned"], t)
                dve.tensor_tensor(ag[:, :], a_in[:, s, :], g_attn[:, :], ALU.mult).then_inc(S["ag_done"], 1)

            def front_rest(t, s):
                dve.wait_ge(S["a_hi_done"], t + 1)
                dve.tensor_tensor(a_lo[:, s], t_bank[:, :].rearrange("p (j n) -> p j n", j=CJ), a_hi[:, s].bitcast(F32),
                                  ALU.subtract).then_inc(S["a_lo_done"], 1)

            def front_variance(t, s):
                dve.wait_ge(S["sq_a"], t + 1)
                dve.wait_ge(S["c_summed"], t + 1)
                dve.tensor_scalar(d_ac[:, s, 0:1], s_ac[:, s, 0:1], 1.0 / AD, EPS, ALU.mult, ALU.add)
                dve.tensor_scalar(d_ac[:, s, 1:2], q_bank[:, 0:1], 1.0 / CD, EPS, ALU.mult, ALU.add).then_inc(S["var_ac"], 1)

            def front_root(t, s):
                dve.wait_ge(S["std_ac"], t + 1)
                dve.reciprocal(r_ac[:, s, :], d_ac[:, s, :]).then_inc(S["rstd_ac"], 1)

            def mix(t, s):
                dve.wait_ge(S["c_mult"], t + 1)
                dve.wait_ge(S["part_done"], t + 1)
                dve.scalar_tensor_tensor(mixed[:, :], c_bank[:, :], r_ac[:, s, 1:2], part[:, :], ALU.mult, ALU.add).then_inc(S["mixed_done"], 1)

            def back_norm(t, s):
                dve.wait_ge(S["sq_m"], t + 1)
                dve.tensor_scalar(d_m[:, :], s_m[:, :], 1.0 / D, EPS, ALU.mult, ALU.add).then_inc(S["var_m"], 1)
                dve.wait_ge(S["std_m"], t + 1)
                dve.reciprocal(r_m[:, :], d_m[:, :]).then_inc(S["rstd_m"], 1)
                dve.wait_ge(S["rstd_m"], t + 1)
                dve.scalar_tensor_tensor(scaled[:, :], mixed[:, :], r_m[:, :], g_post[:, :], ALU.mult, ALU.mult).then_inc(S["scaled_done"], 1)
                dve.wait_ge(S["scaled_done"], t + 1)
                dve.wait_ge(x_loaded[s], half_of(t, s))
                if not isinstance(t, int) or t >= 2:
                    dve.wait_ge(x2_stored[s], half_of(t, s) - 16)
                dve.tensor_tensor(x2[:, s, :], scaled[:, :], x_in[:, s, :], ALU.add).then_inc(S["x2_done"], 1)

            def back_second(t, s):
                dve.wait_ge(S["sq_2"], t + 1)
                dve.tensor_scalar(d_2[:, :], s_2[:, :], 1.0 / D, EPS, ALU.mult, ALU.add).then_inc(S["var_2"], 1)
                dve.wait_ge(S["std_2"], t + 1)
                dve.reciprocal(r_2[:, :], d_2[:, :]).then_inc(S["rstd_2"], 1)
                dve.wait_ge(S["rstd_2"], t + 1)
                if not isinstance(t, int) or t >= 1:
                    dve.wait_ge(S["h2_turned"], 2 * t)
                dve.scalar_tensor_tensor(h2[:, :], x2[:, s, :], r_2[:, :], g_mlp[:, :], ALU.mult, ALU.mult).then_inc(S["h2_done"], 1)

            def h2_rest(t, s):
                for b in range(2):
                    dve.wait_ge(S["h2_hi_done"], 2 * t + b + 1)
                    dve.tensor_tensor(h2_lo[:, s, 4 * b:4 * b + 4], h_bank[b][:, :].rearrange("p (k n) -> p k n", k=4),
                                      h2_hi[:, s, 4 * b:4 * b + 4].bitcast(F32), ALU.subtract).then_inc(S["h2_lo_done"], 1)

            def w_rest(k):
                dve.wait_ge(S["w_hi_done"], k + 1)
                dve.tensor_tensor(w_lo[:, k, :], w_raw[:, k, :], w_hi[:, k, :].bitcast(F32), ALU.subtract).then_inc(S["w_lo_done"], 1)

            dve.wait_ge(S["g_loaded"], 32)
            scale_rows(0, 0)
            w_rest(0)
            w_rest(1)
            front_rest(0, 0)
            front_variance(0, 0)
            front_root(0, 0)
            for k in range(2, KB):
                w_rest(k)
            dve.wait_ge(S["g_late_loaded"], 32)

            def step(t, s):
                last, nxt = not isinstance(t, int) or t >= 1, is_tile(t + 1)
                if last:
                    mix(t - 1, 1 - s)
                if nxt:
                    scale_rows(t + 1, 1 - s)
                if not isinstance(t, int) or t >= 2:
                    h2_rest(t - 2, s)
                if last:
                    back_norm(t - 1, 1 - s)
                if nxt:
                    front_rest(t + 1, 1 - s)
                    front_variance(t + 1, 1 - s)
                    front_root(t + 1, 1 - s)
                if last:
                    back_second(t - 1, 1 - s)

            run(dve, step)
            h2_rest(RT - 1, (RT - 1) % 2)

        @block.tensor
        def _(pe):
            pe.wait_ge(S["g_loaded"], 32)
            pe.wait_ge(S["ones_done"], 1)
            pe.transpose(q_bank[:, 64:64 + CJ], g_conv_rows[:, :], ident[0:CJ, 0:CJ]).then_inc(S["g_rows_t"], 1)
            pe.wait_ge(S["g_conv_done"], 1)

            def turn(t, s):
                pe.wait_ge(S["ag_done"], t + 1)
                if not isinstance(t, int) or t >= 1:
                    pe.wait_ge(S["a_lo_done"], t)
                for j in range(CJ):
                    tr = pe.transpose(t_bank[:, j * P:(j + 1) * P], ag[:, j * P:(j + 1) * P], ident[:, :])
                tr.then_inc(S["a_turned"], 1)
                pe.wait_ge(S["csq_done"], t + 1)
                if not isinstance(t, int) or t >= 1:
                    pe.wait_ge(S["var_ac"], t)
                for j in range(CJ):
                    mm = pe.matmul(q_bank[:, 0:1], csq[:, j, :], ones[:, :], start=(j == 0), stop=(j == CJ - 1))
                mm.then_inc(S["c_summed"], 1)

            def multiply(bank, hi, lo, s, k0, done):
                for half in range(2):
                    cols = slice(512 * half, 512 * half + 512)
                    for j in range(CJ):
                        for i, (a, w) in enumerate(((hi, w_hi), (hi, w_lo), (lo, w_hi))):
                            mm = pe.matmul(bank[:, cols], a[:, s, j, :], w[:, k0 + j, cols], start=(j == 0 and i == 0), stop=(j == CJ - 1 and i == 2))
                mm.then_inc(done, 1)

            turn(0, 0)

            def step(t, s):
                if is_tile(t):
                    if isinstance(t, int) and t == 0:
                        pe.wait_ge(S["w_lo_done"], CJ)
                    else:
                        pe.wait_ge(S["part_done"], t)
                    pe.wait_ge(S["a_lo_done"], t + 1)
                    multiply(a_bank, a_hi, a_lo, s, 0, S["a_mult"])
                if is_tile(t + 1):
                    turn(t + 1, 1 - s)
                if is_tile(t):
                    if isinstance(t, int) and t == 0:
                        pe.wait_ge(S["w_lo_done"], KB)
                    else:
                        pe.wait_ge(S["mixed_done"], t)
                    pe.wait_ge(S["c_lo_done"], t + 1)
                    multiply(c_bank, c_hi, c_lo, s, CJ, S["c_mult"])
                if not isinstance(t, int) or t >= 1:
                    pe.wait_ge(S["h2_done"], t)
                    for b in range(2):
                        if not isinstance(t, int) or t >= 2:
                            pe.wait_ge(S["h2_lo_done"], 2 * (t - 1) - 1 + b)
                        for k in range(4):
                            tr = pe.transpose(h_bank[b][:, k * P:(k + 1) * P], h2[:, (4 * b + k) * P:(4 * b + k + 1) * P], ident[:, :])
                        tr.then_inc(S["h2_turned"], 1)

            run(pe, step)


def mlp(nc, io, dr, sem):
    FC = 2 * P
    CHUNKS = FF // FC
    PAIRS = CHUNKS // 2
    SUB = 3 * P
    TILES = [range(0, 8), range(8, RT)]
    FIRST_ROW = [r[0] * P for r in TILES]
    SUBS = [(3, 3, 2), (3, 3, 3)]
    WIDTHS = [(SUB, SUB, 2 * P), (SUB, SUB, 2 * P + DEC)]
    STEPS = 3 * CHUNKS

    ctx = ExitStack()
    with ctx:
        def sb(name, shape, dt=F32):
            return ctx.enter_context(nc.sbuf_tensor(name, shape, dt))

        h_hi = sb("m_h_hi", [P, KB, 2 * SUB + 2 * P + DEC], F32R)
        h_lo = sb("m_h_lo", [P, KB, 2 * SUB + 2 * P + DEC], F32R)
        y = sb("y", [P, 9, D])
        w_raw = sb("m_raw", [P, KB * FC])
        up_hi = sb("up_hi", [P, 2, KB, FC], F32R)
        up_lo = sb("up_lo", [P, 2, KB, FC], F32R)
        dn_hi = sb("dn_hi", [P, 2, 2, D], F32R)
        dn_lo = sb("dn_lo", [P, 2, 2, D], F32R)
        u = sb("u", [P, 2, SUB])
        u_hi = sb("u_hi", [P, 2, 2, SUB], F32R)
        u_lo = sb("u_lo", [P, 2, 2, SUB], F32R)
        g_post = sb("m_g_post", [P, D])
        x_in = sb("m_x_in", [P, 2, D])
        junk = sb("m_junk", [P, D])
        ssq, std, rstd = sb("m_ssq", [P, RT]), sb("m_std", [P, RT]), sb("m_rstd", [P, RT])
        up_bank = [ctx.enter_context(nc.psum_tensor(f"up_bank{i}", [P, 512], F32)) for i in range(4)]
        dn_bank = [ctx.enter_context(nc.psum_tensor(f"dn_bank{i}", [P, D], F32)) for i in range(2)]

        h_loaded = [sem(f"m_h_loaded{s}") for s in range(3)]
        w_loaded = sem("m_w_loaded")
        g_loaded = sem("m_g_loaded")
        w_hi_done = sem("m_w_hi_done")
        w_lo_done = sem("m_w_lo_done")
        up_done = sem("m_up_done")
        relu_done = sem("m_relu_done")
        u_hi_done = sem("m_u_hi_done")
        u_done = sem("m_u_done")
        u_lo_done = sem("m_u_lo_done")
        dn_done = sem("m_dn_done")
        y_added = sem("m_y_added")
        sq_done = sem("m_sq_done")
        var_done = sem("m_var_done")
        std_done = sem("m_std_done")
        rstd_done = sem("m_rstd_done")
        scaled = sem("m_scaled")
        out_done = sem("m_out_done")
        x_loaded = [sem(f"m_x_loaded{i}") for i in range(2)]
        y_stored = [sem(f"m_y_stored{i}") for i in range(2)]

        up_view = io["w_up"].rearrange("o (k p) f -> (o p) k f", p=P)
        dn_view = io["w_down"].rearrange("o (f p) d -> (o p) f d", p=P)

        def step_no(i, o):
            return 6 * i + o

        def tiles_before(g, i, o):
            if isinstance(i, int):
                g, n = divmod(6 * i + o, STEPS)
                return (0, 8 * CHUNKS)[g] + (8, 9)[g] * (n // 3) + 3 * (n % 3)
            base = 16 * i if g == 0 else 18 * i - 2 * PAIRS
            return base + (8, 9)[g] * (o // 3) + 3 * (o % 3)

        def run(eng, step):
            for g in range(2):
                for o in range(6):
                    step(g, g * PAIRS, o)
                with eng.Fori(g * PAIRS + 1, (g + 1) * PAIRS - 1) as i:
                    for o in range(6):
                        step(g, i, o)
                for o in range(6):
                    step(g, (g + 1) * PAIRS - 1, o)

        def following(g, i, o):
            if o < 5:
                return g, i, o + 1
            if not isinstance(i, int):
                return g, i, 6
            if i + 1 == 2 * PAIRS:
                return None
            return (i + 1) // PAIRS, i + 1, 0

        def first_chunk(g, i, o):
            return isinstance(i, int) and i == g * PAIRS and o < 3

        def finishing(i, o):
            if isinstance(i, int) and (6 * i + o) % STEPS >= STEPS - 3:
                return (6 * i + o) // STEPS, o % 3
            return None

        def tiles_of(g, s):
            return range(TILES[g][3 * s], TILES[g][3 * s] + SUBS[g][s])

        def parity_of_chunk(o):
            return (o // 3) % 2

        block = ctx.enter_context(nc.Block())

        @block.sync
        def _(sp):
            def load_w(g, i, cc, which):
                n = 4 * i + 2 * cc + which
                if not isinstance(n, int) or n >= 1:
                    sp.wait_ge(w_lo_done, n)
                chunk = 2 * i + cc - g * CHUNKS
                if which == 0:
                    sp.dma_start(w_raw[:, :].rearrange("p (k f) -> p k f", k=KB), up_view[:, :, bass.ds(chunk * FC, FC)]).then_inc(w_loaded, 16)
                else:
                    sp.dma_start(w_raw[:, :].rearrange("p (k f) -> p k f", k=2), dn_view[:, bass.ds(chunk * 2, 2), :]).then_inc(w_loaded, 16)

            def load_x(t):
                if t >= 2:
                    sp.wait_ge(out_done, t - 1)
                n = rows_of(t)
                sp.dma_start(x_in[0:n, t % 2, :], dr["x2"][t * P:t * P + n, :]).then_inc(x_loaded[t % 2], 16)

            def store_y(t):
                sp.wait_ge(out_done, t + 1)
                if t >= 2:
                    sp.wait_ge(y_stored[t % 2], 16 * (t // 2))
                dst = io["y_prompt"][0, t * P:(t + 1) * P, :] if t < QT else io["y_sample"][0]
                sp.dma_start(dst, y[0:rows_of(t), t - (8 if t >= 8 else 0), :]).then_inc(y_stored[t % 2], 16)

            def finish(g, s):
                for t in tiles_of(g, s):
                    store_y(t)
                    if t + 2 < RT:
                        load_x(t + 2)

            load_w(0, 0, 0, 0)
            load_w(0, 0, 0, 1)
            sp.dma_start(g_post[:, :], io["g_post_mlp"].to_broadcast([P, D])).then_inc(g_loaded, 16)
            load_x(0)
            load_x(1)
            load_w(0, 0, 1, 0)
            load_w(0, 0, 1, 1)
            with sp.Fori(1, PAIRS) as i:
                for cc in range(2):
                    for which in range(2):
                        load_w(0, i, cc, which)
            load_w(1, PAIRS, 0, 0)
            load_w(1, PAIRS, 0, 1)
            finish(0, 0)
            load_w(1, PAIRS, 1, 0)
            finish(0, 1)
            finish(0, 2)
            load_w(1, PAIRS, 1, 1)
            with sp.Fori(PAIRS + 1, 2 * PAIRS) as i:
                for cc in range(2):
                    for which in range(2):
                        load_w(1, i, cc, which)
            for s in range(3):
                finish(1, s)
            for i in range(2):
                sp.wait_ge(y_stored[i], 16 * ((RT + 1 - i) // 2))

        @block.gpsimd
        def _(pool):
            def load_h(g, s):
                if g == 1:
                    pool.wait_ge(up_done, 2 * (STEPS - 3 + s + 1))
                w = WIDTHS[g][s]
                rows = slice(FIRST_ROW[g] + s * SUB, FIRST_ROW[g] + s * SUB + w)
                for h, name in ((h_hi, "h2_hi"), (h_lo, "h2_lo")):
                    pool.dma_start(h[:, :, s * SUB:s * SUB + w], dr[name].rearrange("(k p) r -> p k r", p=P)[:, :, rows]).then_inc(h_loaded[s], 16)

            def split_rest(g, i, o, which):
                n = 4 * i + 2 * (o // 3) + which
                hi, lo = (up_hi, up_lo) if which == 0 else (dn_hi, dn_lo)
                c = parity_of_chunk(o)
                pool.wait_ge(w_hi_done, n + 1)
                pool.tensor_tensor(lo[:, c], w_raw[:, :].rearrange("p (k f) -> p k f", k=KB if which == 0 else 2),
                                   hi[:, c].bitcast(F32), ALU.subtract).then_inc(w_lo_done, 1)

            def hidden_rest(g, i, o):
                n, w = step_no(i, o), WIDTHS[g][o % 3]
                for b in range(2):
                    pool.wait_ge(u_done, 2 * n + b + 1)
                    pool.tensor_tensor(u_lo[:, o % 2, b, 0:w], u[:, b, 0:w], u_hi[:, o % 2, b, 0:w].bitcast(F32), ALU.subtract).then_inc(u_lo_done, 1)

            for s in range(3):
                load_h(0, s)
            split_rest(0, 0, 0, 0)
            split_rest(0, 0, 0, 1)
            hidden_rest(0, 0, 0)

            def step(g, i, o):
                nxt = following(g, i, o)
                if nxt:
                    hidden_rest(*nxt)
                if isinstance(i, int) and i == PAIRS - 1 and o >= 2 and nxt and (nxt[0] == 0):
                    load_h(1, o - 2)
                if o % 3 < 2 and not (isinstance(i, int) and i == 2 * PAIRS - 1 and o >= 3):
                    split_rest(g, i, o + 3, o % 3)

            run(pool, step)

        @block.scalar
        def _(act):
            def split_first(g, i, o, which):
                n = 4 * i + 2 * (o // 3) + which
                hi = up_hi if which == 0 else dn_hi
                c = parity_of_chunk(o)
                act.wait_ge(w_loaded, 16 * (n + 1))
                if not isinstance(n, int) or n >= 4:
                    if which == 0:
                        act.wait_ge(up_done, 2 * (step_no(i, o // 3 * 3) - 3))
                    else:
                        act.wait_ge(dn_done, tiles_before(g, i, o // 3 * 3 - 3))
                act.activation(hi[:, c], w_raw[:, :].rearrange("p (k f) -> p k f", k=KB if which == 0 else 2), ACT.Copy).then_inc(w_hi_done, 1)

            def hidden_first(g, i, o):
                n, w = step_no(i, o), WIDTHS[g][o % 3]
                if not isinstance(n, int) or n >= 2:
                    act.wait_ge(dn_done, tiles_before(g, i, o - 1))
                for b in range(2):
                    act.wait_ge(up_done, 2 * n + b + 1)
                    if not isinstance(n, int) or n >= 1:
                        act.wait_ge(u_lo_done, 2 * n + b - 1)
                    act.activation(u[:, b, 0:w], up_bank[2 * (o % 2) + b][:, 0:w], ACT.Relu).then_inc(relu_done, 1)
                for b in range(2):
                    act.wait_ge(relu_done, 2 * n + b + 1)
                    act.activation(u_hi[:, o % 2, b, 0:w], u[:, b, 0:w], ACT.Square).then_inc(u_hi_done, 1)

            def square(t):
                act.wait_ge(y_added, (8 * CHUNKS if t < 8 else 17 * CHUNKS) - (TILES[t // 8 if t < 8 else 1][-1] - t))
                if t >= 1:
                    act.wait_ge(sq_done, t)
                act.activation(junk[:, :], y[:, t - (8 if t >= 8 else 0), :], ACT.Square, accum_out=ssq[:, t:t + 1]).then_inc(sq_done, 1)

            def root(t):
                act.wait_ge(var_done, t + 1)
                act.activation(std[:, t:t + 1], std[:, t:t + 1], ACT.Sqrt).then_inc(std_done, 1)

            def finish(g, s):
                tiles = tiles_of(g, s)
                for t in tiles:
                    square(t)
                    if t > tiles[0]:
                        root(t - 1)
                root(tiles[-1])

            split_first(0, 0, 0, 0)
            split_first(0, 0, 0, 1)
            hidden_first(0, 0, 0)

            def step(g, i, o):
                nxt = following(g, i, o)
                if nxt:
                    hidden_first(*nxt)
                if o % 3 < 2 and not (isinstance(i, int) and i == 2 * PAIRS - 1 and o >= 3):
                    split_first(g, i, o + 3, o % 3)
                if finishing(i, o):
                    finish(*finishing(i, o))

            run(act, step)

        @block.vector
        def _(dve):
            def hidden(g, i, o):
                n, w = step_no(i, o), WIDTHS[g][o % 3]
                for b in range(2):
                    dve.wait_ge(u_hi_done, 2 * n + b + 1)
                    dve.tensor_tensor(u[:, b, 0:w], u[:, b, 0:w], u[:, b, 0:w], ALU.mult).then_inc(u_done, 1)

            def add(g, i, o):
                before = tiles_before(g, i, o)
                for k in range(SUBS[g][o % 3]):
                    tile = 3 * (o % 3) + k
                    bank = dn_bank[((9 if g else 8) * (o // 3) + tile) % 2]
                    if first_chunk(g, i, o) and g == 1:
                        t = tile
                        if t < 8:
                            dve.wait_ge(y_stored[t % 2], 16 * (t // 2 + 1))
                    dve.wait_ge(dn_done, before + k + 1)
                    if first_chunk(g, i, o):
                        dve.tensor_copy(y[:, tile, :], bank[:, :]).then_inc(y_added, 1)
                    else:
                        dve.tensor_tensor(y[:, tile, :], bank[:, :], y[:, tile, :], ALU.add).then_inc(y_added, 1)

            def variance(t):
                dve.wait_ge(sq_done, t + 1)
                dve.tensor_scalar(std[:, t:t + 1], ssq[:, t:t + 1], 1.0 / D, EPS, ALU.mult, ALU.add).then_inc(var_done, 1)

            def finish(g, s):
                for t in tiles_of(g, s):
                    variance(t)
                    place = y[:, t - (8 if t >= 8 else 0), :]
                    dve.wait_ge(std_done, t + 1)
                    dve.reciprocal(rstd[:, t:t + 1], std[:, t:t + 1]).then_inc(rstd_done, 1)
                    dve.wait_ge(rstd_done, t + 1)
                    dve.scalar_tensor_tensor(place, place, rstd[:, t:t + 1], g_post[:, :], ALU.mult, ALU.mult).then_inc(scaled, 1)
                    dve.wait_ge(scaled, t + 1)
                    dve.wait_ge(x_loaded[t % 2], 16 * (t // 2 + 1))
                    dve.tensor_tensor(place, place, x_in[:, t % 2, :], ALU.add).then_inc(out_done, 1)

            hidden(0, 0, 0)
            dve.wait_ge(g_loaded, 16)

            def step(g, i, o):
                nxt = following(g, i, o)
                if nxt:
                    hidden(*nxt)
                add(g, i, o)
                if finishing(i, o):
                    finish(*finishing(i, o))

            run(dve, step)

        @block.tensor
        def _(pe):
            def up(g, i, o):
                n, c, s = step_no(i, o), parity_of_chunk(o), o % 3
                w = WIDTHS[g][s]
                if s == 0:
                    pe.wait_ge(w_lo_done, 4 * i + 2 * (o // 3) + 1)
                if first_chunk(g, i, o):
                    pe.wait_ge(h_loaded[s], 32 * (g + 1))
                for b in range(2):
                    if not isinstance(n, int) or n >= 2:
                        pe.wait_ge(relu_done, 2 * n + b - 3)
                    for k in range(KB):
                        for p, (wp, hp) in enumerate(((up_hi, h_hi), (up_hi, h_lo), (up_lo, h_hi))):
                            mm = pe.matmul(up_bank[2 * (o % 2) + b][:, 0:w], wp[:, c, k, b * P:(b + 1) * P], hp[:, k, s * SUB:s * SUB + w],
                                           start=(k == 0 and p == 0), stop=(k == KB - 1 and p == 2))
                    mm.then_inc(up_done, 1)

            def down(g, i, o):
                n, c, s = step_no(i, o), parity_of_chunk(o), o % 3
                before = tiles_before(g, i, o)
                if s == 0:
                    pe.wait_ge(w_lo_done, 4 * i + 2 * (o // 3) + 2)
                pe.wait_ge(u_lo_done, 2 * n + 2)
                for k in range(SUBS[g][s]):
                    bank = dn_bank[((9 if g else 8) * (o // 3) + 3 * s + k) % 2]
                    if not isinstance(before, int) or before + k >= 2:
                        pe.wait_ge(y_added, before + k - 1)
                    for half in range(2):
                        cols = slice(512 * half, 512 * half + 512)
                        for b in range(2):
                            for p, (up_, wp) in enumerate(((u_hi, dn_hi), (u_hi, dn_lo), (u_lo, dn_hi))):
                                mm = pe.matmul(bank[:, cols], up_[:, o % 2, b, k * P:(k + 1) * P], wp[:, c, b, cols],
                                               start=(b == 0 and p == 0), stop=(b == 1 and p == 2))
                    mm.then_inc(dn_done, 1)

            up(0, 0, 0)

            def step(g, i, o):
                nxt = following(g, i, o)
                if nxt:
                    up(*nxt)
                down(g, i, o)

            run(pe, step)


def hymba_fox_shortconv_streaming_step_kernel(nc, io):
    def scratch(name, shape):
        return nc.dram_tensor(f"scratch_{name}", shape, F32, kind="Internal").ap()

    ctx = ExitStack()
    with ctx:
        def sem(name):
            return ctx.enter_context(nc.semaphore(name))

        ident = ctx.enter_context(nc.sbuf_tensor("ident", [P, P], F32))
        dr = {
            "q_t": scratch("q_t", [AD, ROWS]),
            "k_t": scratch("k_t", [AD, ROWS]),
            "conv_t": scratch("conv_t", [CD, ROWS]),
            "ncum": scratch("ncum", [HEADS, LKEYS]),
            "attn": scratch("attn", [ROWS, AD]),
            "h2_hi": scratch("h2_hi", [D, ROWS]),
            "h2_lo": scratch("h2_lo", [D, ROWS]),
            "x2": scratch("x2", [ROWS, D]),
        }
        project_inputs(nc, io, dr, sem, ident)
        attend(nc, io, dr, sem, ident)
        mix_rows(nc, io, dr, sem, ident)
        mlp(nc, io, dr, sem)


_INS = ["x_prompt", "x_sample", "cache_k", "cache_v", "cache_logf", "state_conv", "g_pre_mix", "w_in", "b_f", "conv_w",
        "g_attn_out", "g_conv_out", "w_o", "g_post_mix", "g_pre_mlp", "w_up", "w_down", "g_post_mlp"]
_OUTS = [("y_prompt", (1, SEQ, D)), ("y_sample", (1, DEC, D)),
         ("k_prompt", (1, 1, SEQ, HEADS, HD)), ("v_prompt", (1, 1, SEQ, HEADS, HD)), ("logf_prompt", (1, 1, SEQ, HEADS)),
         ("conv_prompt", (1, 1, CONV_W - 1, CD)),
         ("k_sample", (1, 1, DEC, HEADS, HD)), ("v_sample", (1, 1, DEC, HEADS, HD)), ("logf_sample", (1, 1, DEC, HEADS)),
         ("conv_sample", (1, 1, CONV_W - 1, CD))]


def kernel(**inputs):
    import numpy as _np
    import concourse.bacc as _bacc
    from concourse import mybir as _mybir
    from concourse.bass_utils import run_bass_kernel_spmd as _run

    nc = _bacc.Bacc("TRN2", target_bir_lowering=False, num_devices=1)
    arrays, io = {}, {}
    for name in _INS:
        a = _np.ascontiguousarray(inputs[name])
        arrays[f"in_{name}"] = a
        io[name] = nc.dram_tensor(f"in_{name}", a.shape, _mybir.dt.from_np(a.dtype), kind="ExternalInput").ap()
    for name, shape in _OUTS:
        io[name] = nc.dram_tensor(f"out_{name}", shape, _mybir.dt.float32, kind="ExternalOutput").ap()
    hymba_fox_shortconv_streaming_step_kernel(nc, io)
    r = _run(nc, [arrays], core_ids=[0])
    return tuple(r.results[0][f"out_{name}"] for name, _ in _OUTS)
```
